# Optimizing a Trainium2 kernel written in Bass

```python
import math
import jax
import jax.numpy as jnp
from jax import lax
import numpy as np
import jax, jax.numpy as jnp

D_MODEL = 1024
BATCH = 1
SEQ = 256
DEPTH = 1

MEM_LEN = 256
MOBA_HEADS = 8
MOBA_HEAD_DIM = 64
MOBA_BLOCK = 256
MOBA_TOPK = 3
MOBA_Q_CHUNK = 32
RET_HEADS = 4
RET_QK_DIM = 128
RET_V_DIM = 128
RET_CHUNK = 128
ROPE_BASE = 10000.0
MEM_HEADS = 4
MEM_HEAD_DIM = 128
REL_BUCKETS = 32
REL_MAX_DIST = 2048
D_FF = 2816
CONV_WIDTH = 3
EPS = 1e-6
NEG_INF = -1e30

MOBA_W = MOBA_HEADS * MOBA_HEAD_DIM
RET_QK_W = RET_HEADS * RET_QK_DIM
RET_V_W = RET_HEADS * RET_V_DIM
MEM_W = MEM_HEADS * MEM_HEAD_DIM
IN_SIZES = (MOBA_W, MOBA_W, MOBA_W, RET_QK_W, RET_QK_W, RET_V_W, RET_V_W, MEM_W, D_MODEL, D_MODEL, D_MODEL)
IN_SPLIT_AT = tuple(int(s) for s in np.cumsum(IN_SIZES)[:-1])
D_IN = int(sum(IN_SIZES))


def rmsnorm(x, g):
    xf = x.astype(jnp.float32)
    y = xf * lax.rsqrt(jnp.mean(xf * xf, axis=-1, keepdims=True) + EPS)
    return (y * g.astype(jnp.float32)).astype(x.dtype)

def rel_bucket(dist):
    max_exact = REL_BUCKETS // 2
    d = jnp.maximum(dist, 0)
    df = jnp.maximum(d, 1).astype(jnp.float32)
    large = max_exact + (jnp.log(df / max_exact) / math.log(REL_MAX_DIST / max_exact)
                         * (REL_BUCKETS - max_exact)).astype(jnp.int32)
    large = jnp.minimum(large, REL_BUCKETS - 1)
    return jnp.where(d < max_exact, d, large)

def rotary(x, pos):
    half = x.shape[-1] // 2
    inv = ROPE_BASE ** (-jnp.arange(half, dtype=jnp.float32) / half)
    ang = pos.astype(jnp.float32)[:, None] * inv
    cos = jnp.cos(ang)[None, :, None, :]
    sin = jnp.sin(ang)[None, :, None, :]
    x1, x2 = x[..., :half], x[..., half:]
    return jnp.concatenate([x1 * cos - x2 * sin, x1 * sin + x2 * cos], axis=-1).astype(x.dtype)

def moba_attention(q, k, v, rel_bias):
    B, S, H, dh = q.shape
    nb = -(-S // MOBA_BLOCK)
    s_pad = nb * MOBA_BLOCK
    n_sel = min(MOBA_TOPK, nb)
    qc_len = MOBA_Q_CHUNK
    scale = dh ** -0.5
    q = q.transpose(0, 2, 1, 3)
    pad = ((0, 0), (0, 0), (0, s_pad - S), (0, 0))
    k = jnp.pad(k.transpose(0, 2, 1, 3), pad)
    v = jnp.pad(v.transpose(0, 2, 1, 3), pad)
    kb = k.reshape(B, H, nb, MOBA_BLOCK, dh)
    vb = v.reshape(B, H, nb, MOBA_BLOCK, dh)
    k_mean = jnp.mean(kb.astype(jnp.float32), axis=3)

    pos = jnp.arange(S)
    fully_past = jnp.arange(nb)[None, :] < (pos // MOBA_BLOCK)[:, None]
    gate = jnp.einsum('bhsd,bhnd->bhsn', q.astype(jnp.float32), k_mean)
    gate = jnp.where(fully_past, gate, NEG_INF)
    _, sel = lax.top_k(gate, n_sel)

    table = rel_bias.T.astype(jnp.float32)
    b_idx = jnp.arange(B)[:, None, None, None]
    h_idx = jnp.arange(H)[None, :, None, None]
    blk_off = jnp.arange(MOBA_BLOCK)

    def query_chunk(ci):
        c0 = ci * qc_len
        q_pos = c0 + jnp.arange(qc_len)
        blk = c0 // MOBA_BLOCK
        q_c = lax.dynamic_slice_in_dim(q, c0, qc_len, axis=2)
        sel_c = lax.dynamic_slice_in_dim(sel, c0, qc_len, axis=2)
        k_sel = kb[b_idx, h_idx, sel_c]
        v_sel = vb[b_idx, h_idx, sel_c]
        sel_pos = sel_c[..., None] * MOBA_BLOCK + blk_off
        s_sel = jnp.einsum('bhqd,bhqknd->bhqkn', q_c, k_sel).astype(jnp.float32) * scale
        s_sel = s_sel + table[h_idx[..., None], rel_bucket(q_pos[:, None, None] - sel_pos)]
        s_sel = jnp.where((sel_c < blk)[..., None], s_sel, NEG_INF)
        own_start = blk * MOBA_BLOCK
        k_own = lax.dynamic_slice_in_dim(k, own_start, MOBA_BLOCK, axis=2)
        v_own = lax.dynamic_slice_in_dim(v, own_start, MOBA_BLOCK, axis=2)
        d_own = q_pos[:, None] - (own_start + blk_off)[None, :]
        s_own = (jnp.einsum('bhqd,bhnd->bhqn', q_c, k_own).astype(jnp.float32) * scale
                 + table[:, rel_bucket(d_own)])
        s_own = jnp.where(d_own >= 0, s_own, NEG_INF)
        logits = jnp.concatenate([s_sel.reshape(B, H, qc_len, n_sel * MOBA_BLOCK), s_own], axis=-1)
        p = jax.nn.softmax(logits, axis=-1).astype(v.dtype)
        p_sel = p[..., :n_sel * MOBA_BLOCK].reshape(B, H, qc_len, n_sel, MOBA_BLOCK)
        p_own = p[..., n_sel * MOBA_BLOCK:]
        return (jnp.einsum('bhqkn,bhqkne->bhqe', p_sel, v_sel)
                + jnp.einsum('bhqn,bhne->bhqe', p_own, v_own))

    out = lax.map(query_chunk, jnp.arange(S // qc_len))
    return out.transpose(1, 0, 3, 2, 4).reshape(B, S, H * dh)

def retention(q, k, v, g, gn_gain):
    B, S, H, dk = q.shape
    dv = v.shape[-1]
    C = RET_CHUNK
    N = S // C
    pos = jnp.arange(S)
    q = rotary(q, pos)
    k = rotary(k, pos) * (dk ** -0.5)
    log_gamma = jnp.log1p(-jnp.power(2.0, -5.0 - jnp.arange(H, dtype=jnp.float32)))
    i = jnp.arange(C, dtype=jnp.float32)
    diff = i[:, None] - i[None, :]
    decay = jnp.where(diff >= 0, jnp.exp(log_gamma[:, None, None] * jnp.maximum(diff, 0.0)), 0.0)
    q_in = jnp.exp(log_gamma[:, None] * (i + 1.0))
    k_out = jnp.exp(log_gamma[:, None] * (C - 1.0 - i))
    chunk_decay = jnp.exp(log_gamma * C)

    def to_chunks(t):
        return t.reshape(B, N, C, H, t.shape[-1]).transpose(0, 3, 1, 2, 4)
    qc, kc, vc = to_chunks(q), to_chunks(k), to_chunks(v)
    scores = jnp.einsum('bhncd,bhnjd->bhncj', qc, kc) * decay[None, :, None]
    inner = jnp.einsum('bhncj,bhnje->bhnce', scores, vc)
    kv = jnp.einsum('bhnjd,bhnje->nbhde', kc * k_out[None, :, None, :, None], vc).astype(jnp.float32)

    def step(state, kv_n):
        return chunk_decay[None, :, None, None] * state + kv_n, state
    _, prev = lax.scan(step, jnp.zeros((B, H, dk, dv), jnp.float32), kv)
    cross = jnp.einsum('bhncd,nbhde->bhnce', qc * q_in[None, :, None, :, None], prev)
    y = (inner + cross).astype(jnp.float32).transpose(0, 2, 3, 1, 4).reshape(B, S, H, dv)
    mu = jnp.mean(y, axis=-1, keepdims=True)
    var = jnp.mean(jnp.square(y - mu), axis=-1, keepdims=True)
    yn = ((y - mu) * lax.rsqrt(var + EPS)).reshape(B, S, H * dv) * gn_gain.astype(jnp.float32)
    return (yn * jax.nn.silu(g.astype(jnp.float32))).astype(v.dtype)

def memory_attention(q, mem_n, w_mem_kv):
    B, S, H, dh = q.shape
    M = mem_n.shape[1]
    k, v = jnp.split(mem_n @ w_mem_kv, 2, axis=-1)
    k = k.reshape(B, M, H, dh)
    v = v.reshape(B, M, H, dh)
    s = jnp.einsum('bshd,bmhd->bhsm', q, k).astype(jnp.float32) * (dh ** -0.5)
    p = jax.nn.softmax(s, axis=-1).astype(v.dtype)
    return jnp.einsum('bhsm,bmhd->bshd', p, v).reshape(B, S, H * dh)

def conv_ffn(x, w_up, conv_w, conv_b, w_down):
    h = x @ w_up
    c = h.shape[-1]
    h = lax.conv_general_dilated(
        h, conv_w.reshape(CONV_WIDTH, 1, c).astype(h.dtype), window_strides=(1,),
        padding=[(CONV_WIDTH - 1, 0)], dimension_numbers=('NWC', 'WIO', 'NWC'),
        feature_group_count=c) + conv_b
    gate, up = jnp.split(h, 2, axis=-1)
    return (jax.nn.gelu(gate, approximate=False) * up) @ w_down

def first_inputs(seed: int = 0) -> dict:
    key = jax.random.key(seed)
    ks = jax.random.split(key, 18)
    f32 = jnp.float32
    L = DEPTH

    def dense(k, shape, fan_in):
        return jax.random.normal(k, shape, f32) * fan_in ** -0.5

    def gain(k, shape):
        return 1.0 + 0.02 * jax.random.normal(k, shape, f32)

    return {
        "x": jax.random.normal(ks[0], (BATCH, SEQ, D_MODEL), f32),
        "mem": jax.random.normal(ks[1], (BATCH, MEM_LEN, D_MODEL), f32),
        "g_mix": gain(ks[2], (L, D_MODEL)),
        "w_in": dense(ks[3], (L, D_MODEL, D_IN), D_MODEL),
        "rel_bias": 0.5 * jax.random.normal(ks[4], (REL_BUCKETS, MOBA_HEADS), f32),
        "ret_gn_gain": gain(ks[5], (L, RET_V_W)),
        "g_mem": gain(ks[6], (L, D_MODEL)),
        "w_mem_kv": dense(ks[7], (L, D_MODEL, 2 * MEM_W), D_MODEL),
        "w_br_attn": dense(ks[8], (L, MOBA_W, D_MODEL), MOBA_W),
        "w_br_ret": dense(ks[9], (L, RET_V_W, D_MODEL), RET_V_W),
        "w_br_mem": dense(ks[10], (L, MEM_W, D_MODEL), MEM_W),
        "w_out": dense(ks[11], (L, D_MODEL, D_MODEL), D_MODEL),
        "g_ffn": gain(ks[12], (L, D_MODEL)),
        "w_up": dense(ks[13], (L, D_MODEL, 2 * D_FF), D_MODEL),
        "conv_w": dense(ks[14], (L, CONV_WIDTH, 2 * D_FF), CONV_WIDTH),
        "conv_b": 0.02 * jax.random.normal(ks[15], (L, 2 * D_FF), f32),
        "w_down": dense(ks[16], (L, D_FF, D_MODEL), D_FF),
        "g_final": gain(ks[17], (D_MODEL,)),
    }

def first_block(x, mem, g_mix, w_in, rel_bias, ret_gn_gain, g_mem, w_mem_kv, w_br_attn, w_br_ret,
              w_br_mem, w_out, g_ffn, w_up, conv_w, conv_b, w_down, g_final):
    B, S, _ = x.shape
    h = x
    for l in range(DEPTH):
        n = rmsnorm(h, g_mix[l])
        (q_a, k_a, v_a, q_r, k_r, v_r, g_r, q_m, z_a, z_r, z_m) = jnp.split(n @ w_in[l], IN_SPLIT_AT, axis=-1)
        y_a = moba_attention(q_a.reshape(B, S, MOBA_HEADS, MOBA_HEAD_DIM),
                             k_a.reshape(B, S, MOBA_HEADS, MOBA_HEAD_DIM),
                             v_a.reshape(B, S, MOBA_HEADS, MOBA_HEAD_DIM), rel_bias)
        y_r = retention(q_r.reshape(B, S, RET_HEADS, RET_QK_DIM),
                        k_r.reshape(B, S, RET_HEADS, RET_QK_DIM),
                        v_r.reshape(B, S, RET_HEADS, RET_V_DIM), g_r, ret_gn_gain[l])
        y_m = memory_attention(q_m.reshape(B, S, MEM_HEADS, MEM_HEAD_DIM),
                               rmsnorm(mem, g_mem[l]), w_mem_kv[l])
        merged = (jax.nn.sigmoid(z_a) * (y_a @ w_br_attn[l])
                  + jax.nn.sigmoid(z_r) * (y_r @ w_br_ret[l])
                  + jax.nn.sigmoid(z_m) * (y_m @ w_br_mem[l]))
        h = h + merged @ w_out[l]
        h = h + conv_ffn(rmsnorm(h, g_ffn[l]), w_up[l], conv_w[l], conv_b[l], w_down[l])
    return rmsnorm(h, g_final)


DEPTH_2 = 2

CHUNK = 64
RMS_EPS = 1e-6
M_HEADS = 4
M_HEAD_DIM = D_MODEL // 4
M_WIDTH = M_HEADS * M_HEAD_DIM
CONV_K = 4
P_GROUPS = 4
P_WINDOWS = (2, 4, 8, 16)
P_GROUP_DIM = D_MODEL // 4
P_WIDTH = P_GROUPS * P_GROUP_DIM
A_IN = 3 * M_WIDTH + 2 * M_HEADS + 2 * P_WIDTH
A_OUT_IN = M_WIDTH + P_WIDTH
C_HEADS = 8
QK_NOPE = 128
QK_ROPE = 64
QK_HEAD = QK_NOPE + QK_ROPE
V_HEAD = 128
Q_LORA = 384
KV_LORA = 256
C_WIDTH = C_HEADS * V_HEAD
C_IN = Q_LORA + KV_LORA + QK_ROPE + C_WIDTH
ROPE_THETA = 10000.0
Q_BLOCK = 128
N_A = (DEPTH_2 + 1) // 2
N_C = DEPTH_2 // 2


def rms_norm(x, g):
    xf = x.astype(jnp.float32)
    y = xf * lax.rsqrt(jnp.mean(xf * xf, axis=-1, keepdims=True) + RMS_EPS)
    return (y * g.astype(jnp.float32)).astype(x.dtype)

def causal_conv(x, w, b):
    y = lax.conv_general_dilated(x, w[:, None, :].astype(x.dtype), window_strides=(1,),
                                 padding=[(CONV_K - 1, 0)],
                                 dimension_numbers=('NWC', 'WIO', 'NWC'),
                                 feature_group_count=x.shape[-1])
    return y + b

def mlstm_chunkwise(q, k, v, i_pre, log_f):
    B, H, S, Dk = q.shape
    Dv = v.shape[-1]
    nc = S // CHUNK

    def to_chunks(a):
        return jnp.moveaxis(a.reshape(B, H, nc, CHUNK, *a.shape[3:]), 2, 0)

    xs = (to_chunks(q), to_chunks(k), to_chunks(v), to_chunks(i_pre), to_chunks(log_f))
    tri = jnp.tril(jnp.ones((CHUNK, CHUNK), dtype=bool))

    def step(carry, inp):
        C, n, m = carry
        qb, kb, vb, ib, fb = inp
        bcum = jnp.cumsum(fb, axis=-1)
        dmat = jnp.where(tri, bcum[..., :, None] - bcum[..., None, :] + ib[..., None, :], -jnp.inf)
        inter = bcum + m[..., None]
        m_t = jnp.maximum(inter, jnp.max(dmat, axis=-1))
        w_inter = jnp.exp(inter - m_t)
        s = jnp.einsum('bhtd,bhsd->bhts', qb, kb) * jnp.exp(dmat - m_t[..., None])
        num = jnp.einsum('bhts,bhsv->bhtv', s, vb) + w_inter[..., None] * jnp.einsum('bhtd,bhdv->bhtv', qb, C)
        den = jnp.sum(s, axis=-1) + w_inter * jnp.einsum('bhtd,bhd->bht', qb, n)
        h = num / jnp.maximum(jnp.abs(den), jnp.exp(-m_t))[..., None]
        b_last = bcum[..., -1]
        g = b_last[..., None] - bcum + ib
        m_new = jnp.maximum(b_last + m, jnp.max(g, axis=-1))
        ws = jnp.exp(g - m_new[..., None])
        wc = jnp.exp(b_last + m - m_new)
        kw = kb * ws[..., None]
        C_new = wc[..., None, None] * C + jnp.einsum('bhsd,bhsv->bhdv', kw, vb)
        n_new = wc[..., None] * n + jnp.sum(kw, axis=2)
        return (C_new, n_new, m_new), h

    init = (jnp.zeros((B, H, Dk, Dv), jnp.float32), jnp.zeros((B, H, Dk), jnp.float32),
            jnp.zeros((B, H), jnp.float32))
    _, hs = lax.scan(step, init, xs)
    return jnp.moveaxis(hs, 0, 2).reshape(B, H, S, Dv)

def multiscale_pool(xp):
    B, S, _ = xp.shape
    xf = xp.astype(jnp.float32)
    cs = jnp.pad(jnp.cumsum(xf, axis=1), ((0, 0), (1, 0), (0, 0)))
    t = jnp.arange(S)
    means = []
    for g, w in enumerate(P_WINDOWS):
        csg = cs[..., g * P_GROUP_DIM:(g + 1) * P_GROUP_DIM]
        lo = jnp.maximum(t + 1 - w, 0)
        cnt = jnp.minimum(t + 1, w).astype(jnp.float32)
        means.append((csg[:, 1:] - jnp.take(csg, lo, axis=1)) / cnt[None, :, None])
    return (jnp.concatenate(means, axis=-1) - xf).astype(xp.dtype)

def mlstm_pool_layer(x, norm_g, w_in, b_if, conv_w, conv_b, w_q, w_k, w_v, head_norm_g, skip,
                     pool_w, pool_scale, w_out):
    B, S, _ = x.shape
    u = rms_norm(x, norm_g) @ w_in
    s1 = M_WIDTH
    s2 = 2 * M_WIDTH
    s3 = s2 + 2 * M_HEADS
    s4 = s3 + M_WIDTH
    s5 = s4 + P_WIDTH
    xm, om, gates, zm, xp, zp = jnp.split(u, [s1, s2, s3, s4, s5], axis=-1)
    xc = jax.nn.silu(causal_conv(xm, conv_w, conv_b))
    xc_h = xc.reshape(B, S, M_HEADS, M_HEAD_DIM)
    xm_h = xm.reshape(B, S, M_HEADS, M_HEAD_DIM)
    q = jnp.einsum('bshc,hcd->bhsd', xc_h, w_q).astype(jnp.float32)
    k = jnp.einsum('bshc,hcd->bhsd', xc_h, w_k).astype(jnp.float32) * (M_HEAD_DIM ** -0.5)
    v = jnp.einsum('bshc,hcd->bhsd', xm_h, w_v).astype(jnp.float32)
    gates = (gates + b_if).astype(jnp.float32)
    i_pre = jnp.moveaxis(gates[..., :M_HEADS], -1, 1)
    log_f = jnp.moveaxis(jax.nn.log_sigmoid(gates[..., M_HEADS:]), -1, 1)
    hm = mlstm_chunkwise(q, k, v, i_pre, log_f)
    hm = jnp.moveaxis(hm, 1, 2).reshape(B, S, M_WIDTH).astype(x.dtype) * jax.nn.sigmoid(om)
    hm = rms_norm(hm.reshape(B, S, M_HEADS, M_HEAD_DIM),
                  head_norm_g.reshape(M_HEADS, M_HEAD_DIM)).reshape(B, S, M_WIDTH)
    ya = (hm + skip * xc) * jax.nn.silu(zm)
    mix = multiscale_pool(xp).reshape(B, S, P_GROUPS, P_GROUP_DIM)
    yb = jnp.einsum('bsgc,gcd->bsgd', mix, pool_w).reshape(B, S, P_WIDTH) * pool_scale * jax.nn.silu(zp)
    return x + jnp.concatenate([ya, yb], axis=-1) @ w_out

def rope(x, cos, sin):
    x1, x2 = jnp.split(x.astype(jnp.float32), 2, axis=-1)
    return jnp.concatenate([x1 * cos - x2 * sin, x2 * cos + x1 * sin], axis=-1).astype(x.dtype)

def block_causal_attention(q, k, v):
    B, S, H, _ = q.shape
    scale = QK_HEAD ** -0.5
    chunk_id = jnp.arange(S) // CHUNK
    outs = []
    for qb in range(S // Q_BLOCK):
        q0, q1 = qb * Q_BLOCK, (qb + 1) * Q_BLOCK
        s = jnp.einsum('bqhd,bkhd->bhqk', q[:, q0:q1], k[:, :q1],
                       preferred_element_type=jnp.float32) * scale
        mask = chunk_id[q0:q1, None] >= chunk_id[None, :q1]
        p = jax.nn.softmax(jnp.where(mask, s, -jnp.inf), axis=-1).astype(v.dtype)
        outs.append(jnp.einsum('bhqk,bkhd->bqhd', p, v[:, :q1]))
    return jnp.concatenate(outs, axis=1)

def mla_layer(x, positions, norm_g, w_in, q_norm_g, kv_norm_g, w_uq, w_ukv, qn_g, kn_g, w_out):
    B, S, _ = x.shape
    u = rms_norm(x, norm_g) @ w_in
    cq, ckv, kpe, z = jnp.split(u, [Q_LORA, Q_LORA + KV_LORA, Q_LORA + KV_LORA + QK_ROPE], axis=-1)
    q = (rms_norm(cq, q_norm_g) @ w_uq).reshape(B, S, C_HEADS, QK_HEAD)
    kv = (rms_norm(ckv, kv_norm_g) @ w_ukv).reshape(B, S, C_HEADS, QK_NOPE + V_HEAD)
    k_nope, v = jnp.split(kv, [QK_NOPE], axis=-1)
    k = jnp.concatenate([k_nope, jnp.broadcast_to(kpe[:, :, None, :], (B, S, C_HEADS, QK_ROPE))], axis=-1)
    q = rms_norm(q, qn_g)
    k = rms_norm(k, kn_g)
    inv_freq = ROPE_THETA ** (-jnp.arange(0, QK_ROPE, 2, dtype=jnp.float32) / QK_ROPE)
    ang = positions.astype(jnp.float32)[..., None] * inv_freq
    cos = jnp.cos(ang)[:, :, None, :]
    sin = jnp.sin(ang)[:, :, None, :]
    q = jnp.concatenate([q[..., :QK_NOPE], rope(q[..., QK_NOPE:], cos, sin)], axis=-1)
    k = jnp.concatenate([k[..., :QK_NOPE], rope(k[..., QK_NOPE:], cos, sin)], axis=-1)
    o = block_causal_attention(q, k, v).reshape(B, S, C_WIDTH) * jax.nn.silu(z)
    return x + o @ w_out

def second_inputs(seed: int = 0) -> dict:
    key = jax.random.key(seed)
    ks = list(jax.random.split(key, 32))
    f32 = jnp.float32

    def normal(shape, scale):
        return jax.random.normal(ks.pop(), shape, f32) * scale

    def gain(shape):
        return 1.0 + normal(shape, 0.02)

    x = normal((BATCH, SEQ, D_MODEL), 1.0)
    offsets = jax.random.randint(ks.pop(), (BATCH, 1), 0, 64) * CHUNK
    positions = (offsets + jnp.arange(SEQ)[None, :]).astype(jnp.int32)
    a_b_if = jnp.concatenate([normal((N_A, M_HEADS), 0.1),
                              jnp.linspace(3.0, 6.0, M_HEADS)[None, :] + normal((N_A, M_HEADS), 0.1)], axis=-1)
    return {
        'x': x,
        'positions': positions,
        'a_norm_g': gain((N_A, D_MODEL)),
        'a_w_in': normal((N_A, D_MODEL, A_IN), D_MODEL ** -0.5),
        'a_b_if': a_b_if,
        'a_conv_w': normal((N_A, CONV_K, M_WIDTH), CONV_K ** -0.5),
        'a_conv_b': normal((N_A, M_WIDTH), 0.02),
        'a_w_q': normal((N_A, M_HEADS, M_HEAD_DIM, M_HEAD_DIM), M_HEAD_DIM ** -0.5),
        'a_w_k': normal((N_A, M_HEADS, M_HEAD_DIM, M_HEAD_DIM), M_HEAD_DIM ** -0.5),
        'a_w_v': normal((N_A, M_HEADS, M_HEAD_DIM, M_HEAD_DIM), M_HEAD_DIM ** -0.5),
        'a_head_norm_g': gain((N_A, M_WIDTH)),
        'a_skip': gain((N_A, M_WIDTH)),
        'a_pool_w': normal((N_A, P_GROUPS, P_GROUP_DIM, P_GROUP_DIM), P_GROUP_DIM ** -0.5),
        'a_pool_scale': 1.0 + normal((N_A, P_WIDTH), 0.1),
        'a_w_out': normal((N_A, A_OUT_IN, D_MODEL), A_OUT_IN ** -0.5),
        'c_norm_g': gain((N_C, D_MODEL)),
        'c_w_in': normal((N_C, D_MODEL, C_IN), D_MODEL ** -0.5),
        'c_q_norm_g': gain((N_C, Q_LORA)),
        'c_kv_norm_g': gain((N_C, KV_LORA)),
        'c_w_uq': normal((N_C, Q_LORA, C_HEADS * QK_HEAD), Q_LORA ** -0.5),
        'c_w_ukv': normal((N_C, KV_LORA, C_HEADS * (QK_NOPE + V_HEAD)), KV_LORA ** -0.5),
        'c_qn_g': gain((N_C, QK_HEAD)),
        'c_kn_g': gain((N_C, QK_HEAD)),
        'c_w_out': normal((N_C, C_WIDTH, D_MODEL), C_WIDTH ** -0.5),
    }

def second_block(x, positions, a_norm_g, a_w_in, a_b_if, a_conv_w, a_conv_b, a_w_q, a_w_k, a_w_v,
              a_head_norm_g, a_skip, a_pool_w, a_pool_scale, a_w_out, c_norm_g, c_w_in,
              c_q_norm_g, c_kv_norm_g, c_w_uq, c_w_ukv, c_qn_g, c_kn_g, c_w_out):
    for layer in range(DEPTH_2):
        j = layer // 2
        if layer % 2 == 0:
            x = mlstm_pool_layer(x, a_norm_g[j], a_w_in[j], a_b_if[j], a_conv_w[j], a_conv_b[j],
                                 a_w_q[j], a_w_k[j], a_w_v[j], a_head_norm_g[j], a_skip[j],
                                 a_pool_w[j], a_pool_scale[j], a_w_out[j])
        else:
            x = mla_layer(x, positions, c_norm_g[j], c_w_in[j], c_q_norm_g[j], c_kv_norm_g[j],
                          c_w_uq[j], c_w_ukv[j], c_qn_g[j], c_kn_g[j], c_w_out[j])
    return x


def setup_inputs(seed=0):
    out = dict(first_inputs(seed))
    for name, value in second_inputs(seed + 1).items():
        if name != "x":
            out[name + "_2"] = value
    return out


def reference(
    x, mem, g_mix, w_in, rel_bias, ret_gn_gain, g_mem, w_mem_kv, w_br_attn, w_br_ret, w_br_mem,
    w_out, g_ffn, w_up, conv_w, conv_b, w_down, g_final, positions_2, a_norm_g_2, a_w_in_2,
    a_b_if_2, a_conv_w_2, a_conv_b_2, a_w_q_2, a_w_k_2, a_w_v_2, a_head_norm_g_2, a_skip_2,
    a_pool_w_2, a_pool_scale_2, a_w_out_2, c_norm_g_2, c_w_in_2, c_q_norm_g_2, c_kv_norm_g_2,
    c_w_uq_2, c_w_ukv_2, c_qn_g_2, c_kn_g_2, c_w_out_2,
):
    x = first_block(
        x, mem, g_mix, w_in, rel_bias, ret_gn_gain, g_mem, w_mem_kv, w_br_attn, w_br_ret,
        w_br_mem, w_out, g_ffn, w_up, conv_w, conv_b, w_down, g_final,
    )
    return second_block(
        x, positions_2, a_norm_g_2, a_w_in_2, a_b_if_2, a_conv_w_2, a_conv_b_2, a_w_q_2,
        a_w_k_2, a_w_v_2, a_head_norm_g_2, a_skip_2, a_pool_w_2, a_pool_scale_2, a_w_out_2,
        c_norm_g_2, c_w_in_2, c_q_norm_g_2, c_kv_norm_g_2, c_w_uq_2, c_w_ukv_2, c_qn_g_2,
        c_kn_g_2, c_w_out_2,
    )


_drawn_inputs = setup_inputs


def setup_inputs(seed=0):
    import zlib

    import numpy as np

    out = dict(_drawn_inputs(seed))
    spreads = {}
    factors = {'g_mix': 2.688,
     'ret_gn_gain': 5.795,
     'g_mem': 8.0,
     'g_ffn': 2.864,
     'conv_b': 2.73,
     'a_conv_b_2': 4.038,
     'a_head_norm_g_2': 7.662,
     'a_skip_2': 8.0,
     'c_norm_g_2': 8.0,
     'c_q_norm_g_2': 8.0,
     'c_kv_norm_g_2': 8.0,
     'c_qn_g_2': 8.0,
     'c_kn_g_2': 8.0}
    for name, (base, spread) in spreads.items():
        noise = np.random.default_rng([zlib.crc32(name.encode()), seed]).standard_normal(out[name].shape)
        drawn = base * np.exp(spread * noise) if base else spread * noise
        out[name] = jnp.asarray(drawn.astype(out[name].dtype))
    for name, factor in factors.items():
        out[name] = (out[name] * factor).astype(out[name].dtype)
    return out
```

```python
from contextlib import ExitStack

import numpy as np

import concourse.bass as bass
from concourse import mybir

F32 = mybir.dt.float32
F32R = mybir.dt.float32r
I32 = mybir.dt.int32
ALU = mybir.AluOpType
ACT = mybir.ActivationFunctionType
AX = mybir.AxisListType.X

P = 128
D = 1024
S = 256
T = S // P
KB = D // P
PIECE = 2048
RING = 3
EPS = 1e-6
NEG = -1e30
FF = 2816
FB = FF // P
MOBA_H, RET_H, MEM_H, ML_H, MLA_H = 8, 4, 4, 4, 8
TRI = 384

PHASES = [
    ("memkv", 4, 2, "act"), ("qkv", 16, 8, "mix"), ("z", 12, 6, "act"), ("br", 6, 6, "dve"),
    ("wout", 4, 2, "dve"), ("up", 22, 22, "dve"), ("down", 11, 2, "dve"),
    ("xp", 4, 2, "act"), ("zp", 4, 4, "dve"), ("pool", 1, 4, "dve"), ("xm", 4, 4, "dve"),
    ("om", 4, 2, "act"), ("wv", 1, 2, "act"), ("wq", 1, 4, "act"), ("wk", 1, 4, "act"),
    ("zm", 4, 4, "dve"), ("aout", 8, 2, "dve"),
    ("cu", 4, 2, "act"), ("cz0", 2, 1, "dve"), ("uq", 3, 3, "act"), ("ukv", 2, 4, "act"),
    ("cz1", 2, 1, "dve"), ("cout", 4, 2, "dve"),
]
GR = 6


def plan():
    at, first, chunks = 0, {}, []
    count = {"act": 0, "dve": 0}
    parts = 0
    for name, np_, nc_, owner in PHASES:
        first[name] = (at, len(chunks))
        for c in range(nc_):
            o = owner if owner != "mix" else ("dve" if c == GR else "act")
            count[o] += 1
            if nc_ > np_:
                per = nc_ // np_
                end, inside = at + c // per, c % per != per - 1
            elif name in ("down", "aout"):
                end, inside = at + np_ - 1, False
            else:
                end, inside = at + (c + 1) * (np_ // nc_) - 1, False
            parts += inside
            chunks.append((o, count[o], end, parts if inside else None))
        at += np_
    return first, chunks, at


FIRST, CHUNKS, NPIECES = plan()


def p0(name):
    return FIRST[name][0]


def c0(name):
    return FIRST[name][1]


TURNS = [("mem", 8), ("mix", 8), ("ya", 4), ("yr", 4), ("ym", 4), ("merged", 8), ("ffn", 8),
         ("ml", 8), ("mla", 8), ("cq", 5), ("o", 8)]
TURN = {}
_n = 0
for _name, _kb in TURNS:
    TURN[_name] = (_n, _kb)
    _n += (_kb + 1) // 2

PCOL = {}
_n = 0
for _name, _w in [("g_mem", 8), ("g_mix", 8), ("gn", 4), ("g_ffn", 8), ("conv_w", 132), ("conv_b", 44),
                  ("a_norm", 8), ("a_conv_w", 32), ("a_conv_b", 8), ("head_g", 8), ("skip", 8),
                  ("pool_scale", 8), ("c_norm", 8), ("cqkv_norm", 5), ("qn", 1), ("kn", 1),
                  ("qn_pe", 64), ("kn_pe", 64), ("b_i", 1), ("b_f", 1)]:
    PCOL[_name] = (_n, _w)
    _n += _w
NPAR = _n

MOBA0, RET0, MEM0 = 10, 18, 22
ML0 = p0("zm")
NORM_STEP = {"mem": 0, "mix": 2, "merged": p0("wout"), "ffn": p0("up"), "ml": p0("xp"),
             "mla": p0("cu"), "cq": p0("uq") - 1, "o": p0("cout")}
FRONT = {"mix": 1, "cq": p0("cz0")}


XNORMS = ["mem", "mix", "ffn", "ml", "mla", "cq"]
SUMS = ["mem", "mix", "ffn", "final", "ml", "mla", "cq"]


def head_at(n):
    for kind, start, count in (("moba", MOBA0, MOBA_H), ("ret", RET0, RET_H), ("mem", MEM0, MEM_H)):
        if start <= n < start + count:
            return kind, n - start
    return None


def rel_heads(n):
    return {9: (6, 7)}.get(n, (n - 3,) if 3 <= n < 9 else ())


JOBS = [head_at(n) for n in range(MOBA0, MEM0 + MEM_H)]


def job(kind, h):
    return JOBS.index((kind, h))


SMAX = [j for j in range(len(JOBS)) if JOBS[j][0] != "ret"]
TURNED = [j for j in range(len(JOBS)) if JOBS[j][0] != "moba" or JOBS[j][1] % 2 == 0]


def program(nc, ins, out):
    ctx = ExitStack()
    with ctx:
        def sb(name, shape, dt=F32):
            return ctx.enter_context(nc.sbuf_tensor(name, shape, dt))

        def sem(name):
            return ctx.enter_context(nc.semaphore(name))

        def overlay(size, *groups):
            made = []
            for group in groups:
                with ExitStack() as own:
                    made.append([own.enter_context(nc.sbuf_tensor(*g)) for g in group])
            sb(f"overlay_{groups[0][0][0]}", [P, size // 4], F32)
            return made

        raw = sb("raw", [P, RING, PIECE])
        whi = sb("whi", [P, RING, PIECE], F32R)
        wlo = sb("wlo", [P, RING, PIECE], F32R)
        x0hi = sb("x0hi", [P, KB, S], F32R)
        x0lo = sb("x0lo", [P, KB, S], F32R)
        [[x1hi, x1lo], [zm, pe_t, qpe]] = overlay(
            16384, [("x1hi", [P, KB, S], F32R), ("x1lo", [P, KB, S], F32R)],
            [("zm", [P, KB, S], F32), ("pe_t", [P, 2, 4 * P], F32), ("qpe", [P, T, MLA_H, 64], F32)])
        [[tok], [hthi, htlo, gbuf, ubuf, gfin],
         [ybhi, yblo, om, xmhi, xmlo, v_ml, xc], [_1, _2, _3, q_ml, k_ml], [_4, _5, _6, xp, zp],
         [cu, cz, q_c, kv_c, kpe, cqhi, cqlo]] = overlay(
            57344,
            [("tok", [P, 14, T, 512], F32)],
            [("hthi", [P, FB, S], F32R), ("htlo", [P, FB, S], F32R),
             ("gbuf", [P, 2, 2, S], F32), ("ubuf", [P, 2, 2, S], F32), ("gfin", [P, D], F32)],
            [("ybhi", [P, KB, S], F32R), ("yblo", [P, KB, S], F32R), ("om", [P, T, D], F32),
             ("xmhi", [P, KB, S], F32R), ("xmlo", [P, KB, S], F32R), ("v_ml", [P, T, D], F32),
             ("xc", [P, KB, S], F32)],
            [("f1", [P, PIECE], F32), ("f2", [P, PIECE], F32), ("f3", [P, PIECE], F32),
             ("q_ml", [P, KB, S], F32), ("k_ml", [P, KB, S], F32)],
            [("f4", [P, PIECE], F32), ("f5", [P, PIECE], F32), ("f6", [P, PIECE], F32),
             ("xp", [P, T, D], F32), ("zp", [P, KB, S], F32)],
            [("cu", [P, T, 704], F32), ("cz", [P, T, D], F32), ("q_c", [P, T, MLA_H, 192], F32),
             ("kv_c", [P, T, MLA_H, 256], F32), ("kpe", [P, T, MLA_H, 64], F32),
             ("cqhi", [P, 5, S], F32R), ("cqlo", [P, 5, S], F32R)])
        xres = sb("xres", [P, T, D])
        [[xn], [qk_t, prob]] = overlay(
            8192, [("xn", [P, T, D], F32)],
            [("qk_t", [P, 2, 512], F32), ("prob", [P, 2, 512], F32)])
        prob_t = sb("prob_t", [P, 2, 512])
        [[bias, decay, rcos, rsin, onehot, brows], [poolb, mtri, mmla, invf, sel, rows, csin, ccos, ang, kpr]] = overlay(
            8192 + RET_H * TRI * 4 + 1024 + 3 * TRI * 4,
            [("bias", [P, MOBA_H, S], F32), ("decay", [P, RET_H, TRI], F32), ("rcos", [P, T, 64], F32),
             ("rsin", [P, T, 64], F32), ("onehot", [P, TRI], F32), ("brows", [P, 2, TRI], F32)],
            [("poolb", [P, 4, T, S], F32), ("mtri", [P, S], F32), ("mmla", [P, TRI], F32),
             ("invf", [P, 32], F32), ("sel", [P, ML_H, P], F32),
             ("rows", [4, 5, S], F32),
             ("csin", [P, T, 32], F32), ("ccos", [P, T, 32], F32), ("ang", [P, 2, T, 32], F32),
             ("kpr", [P, T, 64], F32)])
        ident = sb("ident", [P, P])
        par = sb("par", [P, NPAR])
        half = sb("half", [P, 20])
        relb = sb("relb", [P, MOBA_H])
        relw = sb("relw", [P, 2, P])
        stats = sb("stats", [P, 32])
        rstd = sb("rstd", [P, 32])
        rs_a = sb("rs_a", [P, 2, 16])
        junk = sb("junk", [P, S])
        nmax = sb("nmax", [P, 4, T])
        psumr = sb("psumr", [P, 4, T])
        rsum = sb("rsum", [P, T])
        bn = sb("bn", [P, T, 6])
        mv = sb("mv", [P, T, 2])
        wgate = sb("wgate", [P, KB, 8])
        wghi = sb("wghi", [P, KB, 8], F32R)
        wglo = sb("wglo", [P, KB, 8], F32R)
        gsb = sb("gsb", [P, T, 8])
        gcol = sb("gcol", [P, 2, T, 4])
        ones = sb("ones", [P, 1])
        posi = sb("posi", [P, T], I32)
        posf = sb("posf", [P, T])
        kss = sb("kss", [P, 2, T, MLA_H])
        kpss = sb("kpss", [P, T])
        rqk = sb("rqk", [P, 2, T, MLA_H])

        hm = [qk_t[:, i, :].rearrange("p (t d) -> p t d", t=T) for i in range(2)]

        ybt = om[:, :, :].rearrange("p t (n s) -> p (t n) s", s=512)

        G = [ctx.enter_context(nc.psum_tensor(f"gemm{i}", [P, 512], F32)) for i in range(4)]
        A = [ctx.enter_context(nc.psum_tensor(f"head{i}", [P, 512], F32)) for i in range(4)]

        s_piece = [sem(f"piece_loaded{i}") for i in range(RING)]
        s_hi = sem("hi_ready")
        s_lo = sem("lo_ready")
        s_mm = sem("piece_multiplied")
        s_part = sem("chunk_in_piece_multiplied")
        s_emptied = {"act": sem("chunk_emptied_by_act"), "dve": sem("chunk_emptied_by_dve")}
        s_act = sem("act_own_order")
        s_dve = sem("dve_own_order")
        s_pool = sem("pool_own_order")
        s_x, s_par, s_mem, s_c1, s_c2, s_gfin, s_pos, s_rel = (sem(n) for n in (
            "x_loaded", "params_loaded", "mem_loaded", "consts1_loaded", "consts2_loaded",
            "gfin_loaded", "positions_loaded", "rel_loaded"))
        s_ss, s_xn, s_turn, s_thi, s_tlo = (sem(n) for n in (
            "squares_summed", "normed", "turned", "turned_hi", "turned_lo"))
        s_rb, s_rbw, s_rbs, s_bias = (sem(n) for n in (
            "rel_rows", "rel_lhs", "rel_rows_copied", "bias_loaded"))
        s_rbd = [sem(f"rel_rows_stored{i}") for i in range(2)]
        s_jt, s_jte, s_js, s_jse, s_jx, s_jp, s_jpe, s_jo, s_jn = (sem(n) for n in (
            "head_turned", "head_turned_copied", "head_scored", "scores_biased", "probs_ready",
            "probs_turned", "probs_turned_copied", "head_weighed", "head_done"))
        s_rot, s_ident, s_half = sem("rotated"), sem("ident_loaded"), sem("halves_ready")
        s_tanh, s_cv, s_gelu, s_h, s_hhi, s_hlo = (sem(n) for n in (
            "tanh_ready", "conv_last_tap", "gelu_ready", "ffn_hidden", "ffn_hidden_hi", "ffn_hidden_lo"))
        s_conv, s_fhi = sem("conv_ready"), sem("form_hi_ready")
        s_gh, s_gl, s_gm, s_gc, s_gt, s_gr, s_gx, s_gct, s_gcol = (sem(n) for n in (
            "gate_weights_hi", "gate_weights_lo", "gates_multiplied", "gates_copied", "gates_turned",
            "gate_rows", "gate_rows_act", "gate_cols_turned", "gate_cols"))
        s_xmlo, s_silu, s_xclo, s_mixm, s_mixhi, s_mixlo, s_yb, s_ybhi, s_yblo = (sem(n) for n in (
            "xm_lo", "xc_tanh", "xc_lo", "pool_mixed", "mix_hi", "mix_lo", "yb_ready", "yb_hi", "yb_lo"))
        s_mo, s_mw, s_mx, s_mp, s_mh, s_mss, s_mn, s_mt, s_mya, s_myhi, s_mylo = (sem(n) for n in (
            "ml_scored", "ml_w", "ml_exp", "ml_probs", "ml_h", "ml_squares", "ml_normed", "ml_turned",
            "ya_ready", "ya_hi", "ya_lo"))
        s_sin, s_ang = sem("sines_ready"), sem("angles_ready")
        s_csq, s_csqr, s_cpe, s_cqk = (sem(n) for n in (
            "mla_squared", "mla_squares_read", "mla_pe_ready", "mla_qk_ready"))
        s_lt, s_ltq, s_ltp, s_ls, s_lse, s_lx, s_lp, s_lpe, s_lo_, s_ln = (sem(n) for n in (
            "mla_turned", "mla_qk_copied", "mla_pe_copied", "mla_scored", "mla_biased", "mla_probs",
            "mla_probs_turned", "mla_probs_copied", "mla_weighed", "mla_done"))
        s_gat = sem("gate_weights_loaded")
        s_rc = sem("rotary_loaded")
        s_zero = sem("zeros_ready")
        s_fin = sem("final_normed")
        s_hm = sem("ml_h_gated")
        s_mskip = sem("ml_skip_scaled")
        s_memset = sem("memset")
        s_store = sem("out_stored")

        scratch = nc.dram_tensor("bias_rows", (MOBA_H, P * TRI), F32, kind="Internal").ap()

        def pcol(name, i=0):
            a = PCOL[name][0] + i
            return par[:, a:a + 1]

        hc = lambda i: half[:, i:i + 1]

        def wait_chunk(eng, c):
            _, _, piece, part = CHUNKS[c]
            if part is None:
                eng.wait_ge(s_mm, piece + 1)
            else:
                eng.wait_ge(s_part, part)

        def chunk_free(eng, c):
            if c >= 0:
                eng.wait_ge(s_emptied[CHUNKS[c][0]], CHUNKS[c][1])

        def bank(c, t=0):
            return G[2 * (c % 2) + t]

        def fills(name):
            base, kb = TURN[name]
            return base, (kb + 1) // 2, kb

        DEST = {"mem": (x1hi, x1lo, 0), "mix": (x0hi, x0lo, 0), "ya": (x1hi, x1lo, 0),
                "yr": (x1hi, x1lo, 4), "ym": (x0hi, x0lo, 0), "merged": (x0hi, x0lo, 0),
                "ffn": (x1hi, x1lo, 0), "ml": (x0hi, x0lo, 0), "mla": (x0hi, x0lo, 0),
                "cq": (cqhi, cqlo, 0), "o": (x0hi, x0lo, 0)}
        GAIN = {"mem": "g_mem", "mix": "g_mix", "ffn": "g_ffn", "ml": "a_norm", "mla": "c_norm",
                "cq": "cqkv_norm"}

        def gain(name, kb):
            if name in GAIN:
                return pcol(GAIN[name], kb)
            if name == "yr":
                return hc(kb)
            return 0.5 if name in ("merged", "o") else 1.0

        def turn_bank(name, i):
            return A[0] if name in ("ya", "yr", "ym") else A[i]

        def turn_source(name, t, kb):
            c = slice(kb * P, kb * P + P)
            if name in ("mem", "mix", "ffn", "ml", "mla", "cq"):
                return xn[:, t, c]
            if name in ("ya", "yr", "ym"):
                return tok[:, {"ya": 0, "yr": 3, "ym": 7}[name], t, c]
            if name == "merged":
                return tok[:, 10 + kb // 4, t, (kb % 4) * P:(kb % 4) * P + P]
            return kv_c[:, t, kb, 0:P]

        def turn_steps(p):
            found = [(n, range(fills(n)[1])) for n, s in NORM_STEP.items() if s == p]
            for n, s in (("ya", 26), ("yr", 28), ("ym", 32)):
                if p in (s, s + 1):
                    found.append((n, [p - s]))
            return found

        block = ctx.enter_context(nc.Block())

        @block.sync
        def _(sp):
            sp.dma_start(tok[:, 12:14, :, :].rearrange("p a b c -> p (a b c)"), ins["mem"]).then_inc(s_mem, 16)
            sp.dma_start(par[:, :], ins["params"]).then_inc(s_par, 16)
            sp.dma_start(ident[:, :], ins["ident"]).then_inc(s_ident, 16)
            for p in range(RING):
                sp.dma_start(raw[:, p, :], ins["weights"][p]).then_inc(s_piece[p], 16)
            rounds = NPIECES // RING
            with sp.Fori(1, rounds) as r:
                for j in range(RING):
                    sp.wait_ge(s_lo, r * RING + (j + 1 - RING))
                    sp.dma_start(raw[:, j, :], ins["weights"][bass.ds(r * RING + j, 1)]
                                 .rearrange("a p n -> p (a n)")).then_inc(s_piece[j], 16)
            for p in range(rounds * RING, NPIECES):
                sp.wait_ge(s_lo, p - RING + 1)
                sp.dma_start(raw[:, p % RING, :], ins["weights"][p]).then_inc(s_piece[p % RING], 16)
            for n in range(2):
                sp.wait_ge(s_emptied["dve"], CHUNKS[c0("cout") + n][1])
                sp.dma_start(out.rearrange("(t p) d -> p t d", p=P)[:, :, n * 512:n * 512 + 512],
                             xres[:, :, n * 512:n * 512 + 512]).then_inc(s_store, 16)
            sp.wait_ge(s_store, 32)

        @block.tensor
        def _(pe):
            mm = nc.tensor.matmul

            def passes(o, xh, xl, wh, wl, start, stop):
                mm(o, xh, wh, start=start, stop=False)
                mm(o, xh, wl, start=False, stop=False)
                return mm(o, xl, wh, start=False, stop=stop)

            def passes_t(o, xh, xl, wh, wl, start, stop):
                mm(o, wh, xh, start=start, stop=False)
                mm(o, wh, xl, start=False, stop=False)
                return mm(o, wl, xh, start=False, stop=stop)

            def piece_ready(p):
                pe.wait_ge(s_lo, p + 1)

            def tokens_piece(p, xh, xl, kbs, banks, width, first, last, col0=0):
                r = p % RING
                for t in range(T):
                    ts = slice(t * P, t * P + P)
                    for j, kb in enumerate(kbs):
                        ws = slice(j * width, (j + 1) * width)
                        i = passes(banks[t][:, col0:col0 + width], xh[:, kb, ts], xl[:, kb, ts],
                                   whi[:, r, ws], wlo[:, r, ws],
                                   first and j == 0, last and j == len(kbs) - 1)
                return i

            def channels_block(r, xh, xl, kbs, off, stride, o):
                for j, kb in enumerate(kbs):
                    ws = slice(off + j * stride, off + j * stride + P)
                    i = passes_t(o, xh[:, kb, :], xl[:, kb, :], whi[:, r, ws], wlo[:, r, ws],
                                 j == 0, j == len(kbs) - 1)
                return i

            def turn(name, which):
                base, n, kbs = fills(name)
                for i in which:
                    if name in XNORMS:
                        pe.wait_ge(s_xn, XNORMS.index(name) + 1)
                    if name == "ya":
                        pe.wait_ge(s_jn, job("moba", MOBA_H - 1) + 1)
                        pe.wait_ge(s_jte, len(TURNED))
                    if name == "yr":
                        pe.wait_ge(s_jn, job("ret", RET_H - 1) + 1)
                    if name == "ym":
                        pe.wait_ge(s_jn, job("mem", MEM_H - 1) + 1)
                    if name == "merged":
                        pe.wait_ge(s_emptied["dve"], CHUNKS[c0("br") + 5][1])
                    if name == "o":
                        pe.wait_ge(s_ln, MLA_H)
                    if base + i >= 1:
                        pe.wait_ge(s_tlo, base + i if name in ("ya", "yr", "ym") else base)
                    if name == "mla":
                        pe.wait_ge(s_mya, ML_H)
                    b = turn_bank(name, i)
                    for j in range(min(2, kbs - 2 * i)):
                        for t in range(T):
                            ins_ = nc.tensor.transpose(b[:, j * S + t * P:j * S + t * P + P],
                                                       turn_source(name, t, 2 * i + j), ident[:, :])
                    ins_.then_inc(s_turn, 1)

            def head_turn(p):
                if head_at(p) is None:
                    return
                kind, h = head_at(p)
                j = job(kind, h)
                if j not in TURNED:
                    return
                n = TURNED.index(j)
                if kind == "moba" and h == 0:
                    chunk_free(pe, c0("qkv") + 2)
                if kind == "ret" and h == 0:
                    pe.wait_ge(s_rot, 1)
                if kind == "mem" and h == 0:
                    chunk_free(pe, c0("qkv") + 7)
                if n >= 1:
                    pe.wait_ge(s_jte, n)
                else:
                    pe.wait_ge(s_tlo, sum(fills("mix")[:2]))
                    pe.wait_ge(s_rbs, MOBA_H)
                qs, ks = {"moba": (0, 1), "ret": (3, 4), "mem": (7, 8)}[kind]
                c = slice((h // 2 if kind == "moba" else h) * P, (h // 2 if kind == "moba" else h) * P + P)
                for i, s_ in enumerate((qs, ks)):
                    for t in range(T):
                        ins_ = nc.tensor.transpose(A[0][:, i * S + t * P:i * S + t * P + P],
                                                   tok[:, s_, t, c], ident[:, :])
                ins_.then_inc(s_jt, 1)

            def turned_buf(j):
                n = max(i for i, m in enumerate(TURNED) if m <= j)
                return n, qk_t[:, n % 2, :]

            def head_score(p):
                if head_at(p - 1) is None:
                    return
                kind, h = head_at(p - 1)
                j = job(kind, h)
                n, qk = turned_buf(j)
                pe.wait_ge(s_jte, n + 1)
                if j >= 1:
                    pe.wait_ge(s_jse, j)
                if kind == "moba":
                    rows_ = slice((h % 2) * 64, (h % 2) * 64 + 64)
                    mm(A[1][:, 0:P], qk[rows_, 0:P], qk[rows_, S:S + P], start=True, stop=True)
                    i = mm(A[1][:, P:P + S], qk[rows_, P:S], qk[rows_, S:2 * S], start=True, stop=True)
                elif kind == "ret":
                    mm(A[1][:, 0:S], qk[:, S:S + P], qk[:, 0:S], start=True, stop=True)
                    i = mm(A[1][:, S:S + P], qk[:, S + P:2 * S], qk[:, P:S], start=True, stop=True)
                else:
                    for t in range(T):
                        i = mm(A[1][:, t * S:t * S + S], qk[:, t * P:t * P + P], qk[:, S:2 * S],
                               start=True, stop=True)
                i.then_inc(s_js, 1)

            def prob_blocks(kind):
                if kind == "mem":
                    return [(t, k, t * S + k * P) for t in range(T) for k in range(T)]
                return [(0, 0, 0), (1, 0, P), (1, 1, 2 * P)]

            def head_prob_turn(p):
                if head_at(p - 2) is None or head_at(p - 2)[0] == "ret":
                    return
                j = job(*head_at(p - 2))
                n = SMAX.index(j)
                pe.wait_ge(s_jx, n + 1)
                if n >= 1:
                    pe.wait_ge(s_jpe, n)
                for i, (t, k, col) in enumerate(prob_blocks(JOBS[j][0])):
                    ins_ = nc.tensor.transpose(A[2][:, i * P:i * P + P], prob[:, j % 2, col:col + P],
                                               ident[:, :])
                ins_.then_inc(s_jp, 1)

            def head_weigh(p):
                if head_at(p - 3) is None:
                    return
                kind, h = head_at(p - 3)
                j = job(kind, h)
                if j >= 1:
                    pe.wait_ge(s_jn, j)
                if kind == "ret":
                    pe.wait_ge(s_jse, j + 1)
                    chunk_free(pe, c0("qkv") + 5)
                    src = [(0, 0, 0), (1, 0, P), (1, 1, 2 * P)]
                    buf, vs, w = prob[:, j % 2, :], 5, P
                else:
                    pe.wait_ge(s_jpe, SMAX.index(j) + 1)
                    src = [(t, k, i * P) for i, (t, k, _) in enumerate(prob_blocks(kind))]
                    buf = prob_t[:, SMAX.index(j) % 2, :]
                    vs, w = (2, 64) if kind == "moba" else (9, P)
                for i, (t, k, col) in enumerate(src):
                    last = mm(A[3][:, t * P:t * P + w], buf[:, col:col + P],
                              tok[:, vs, k, h * w:h * w + w],
                              start=k == 0, stop=i + 1 == len(src) or src[i + 1][0] != t)
                last.then_inc(s_jo, 1)

            def rel_rows(h):
                pe.wait_ge(s_rbw, h + 1)
                if h >= 1:
                    pe.wait_ge(s_rbs, h)
                else:
                    pe.wait_ge(s_c1, 32)
                    pe.wait_ge(s_tlo, sum(fills("mix")[:2]))
                mm(A[3][:, 0:TRI], relw[0:33, h % 2, :], onehot[0:33, :],
                   start=True, stop=True).then_inc(s_rb, 1)

            def gate_logits():
                pe.wait_ge(s_gl, 1)
                pe.wait_ge(s_tlo, sum(fills("ml")[:2]))
                for t in range(T):
                    for kb in range(KB):
                        ts = slice(t * P, t * P + P)
                        i = passes(A[0][:, t * 8:t * 8 + 8], x0hi[:, kb, ts], x0lo[:, kb, ts],
                                   wghi[:, kb, :], wglo[:, kb, :], kb == 0, kb == KB - 1)
                i.then_inc(s_gm, 1)

            def gate_rows():
                pe.wait_ge(s_gc, 1)
                for g in range(2):
                    for t in range(T):
                        i = nc.tensor.transpose(A[1][0:4, g * S + t * P:g * S + t * P + P],
                                                gsb[:, t, g * 4:g * 4 + 4], ident[:, :])
                i.then_inc(s_gt, 1)

            def gate_cols():
                pe.wait_ge(s_gx, 3)
                pe.wait_ge(s_gr, 2)
                for g, row in enumerate((1, 3)):
                    for t in range(T):
                        i = nc.tensor.transpose(A[1][:, (g * T + t) * 4:(g * T + t) * 4 + 4],
                                                rows[0:4, row, t * P:t * P + P], ident[0:4, 0:4])
                i.then_inc(s_gct, 1)

            def pool_mix(p):
                b = p - (p0("pool") - 3)
                if not 0 <= b < 4:
                    return
                if b == 0:
                    pe.wait_ge(s_c2, 80)
                    chunk_free(pe, c0("xp") + 1)
                if b >= 2:
                    pe.wait_ge(s_mixlo, b - 1)
                for j in range(2):
                    cb = 2 * b + j
                    for st in range(T):
                        i = mm(A[2 + b % 2][:, j * S:j * S + S], xp[:, st, cb * P:cb * P + P],
                               poolb[:, cb // 2, st, :], start=st == 0, stop=st == T - 1)
                i.then_inc(s_mixm, 1)

            def ml_weigh(h):
                pe.wait_ge(s_mp, h + 1)
                for t in range(T):
                    for i, st in enumerate(range(t + 1)):
                        col = t * P if st == 0 else S
                        mm(A[3][:, t * S:t * S + S], prob[:, h % 2, col:col + P],
                           v_ml[:, st, h * S:h * S + S], start=i == 0, stop=st == t)
                for t in range(T):
                    for i, st in enumerate(range(t + 1)):
                        col = t * P if st == 0 else S
                        last = mm(A[0][:, 400 + t:401 + t], prob[:, h % 2, col:col + P], ones[:, :],
                                  start=i == 0, stop=st == t)
                return last

            def ml_score(h):
                chunk_free(pe, c0("wk") + h)
                for st in range(T):
                    o = A[1][:, 0:S] if st == 0 else A[1][:, S:S + P]
                    qs = slice(0, S) if st == 0 else slice(P, S)
                    for d in range(2):
                        i = mm(o, k_ml[:, 2 * h + d, st * P:st * P + P], q_ml[:, 2 * h + d, qs],
                               start=d == 0, stop=d == 1)
                return mm(A[0][:, 0:S], sel[0:4, h, :], rows[0:4, 2, :], start=True, stop=True)

            def ml_step(p):
                e = p - ML0
                if not 0 <= e <= ML_H + 1:
                    return
                if e == 0:
                    pe.wait_ge(s_gcol, 1)
                    pe.wait_ge(s_mixlo, 4)
                if e >= 1:
                    pe.wait_ge(s_mp, min(e, ML_H))
                    if e >= 2:
                        pe.wait_ge(s_mh, e - 1)
                if 1 <= e <= ML_H:
                    i = ml_weigh(e - 1)
                if e < ML_H:
                    i = ml_score(e)
                if e <= ML_H:
                    i.then_inc(s_mo, 1)
                if e >= 2:
                    ml_turn(e - 2)

            def ml_turn(h):
                pe.wait_ge(s_mn, h + 1)
                if h >= 1:
                    pe.wait_ge(s_mya, h)
                for j in range(2):
                    for t in range(T):
                        i = nc.tensor.transpose(A[2][:, j * S + t * P:j * S + t * P + P],
                                                hm[h % 2][:, t, j * P:j * P + P], ident[:, :])
                i.then_inc(s_mt, 1)

            def mla_turn(h):
                if h == 0:
                    pe.wait_ge(s_cqk, 1)
                    pe.wait_ge(s_cpe, 1)
                    pe.wait_ge(s_tlo, sum(fills("cq")[:2]))
                else:
                    pe.wait_ge(s_ltq, h)
                for i, (src) in enumerate((q_c, kv_c)):
                    for t in range(T):
                        last = nc.tensor.transpose(A[0][:, i * S + t * P:i * S + t * P + P],
                                                   src[:, t, h, 0:P], ident[:, :])
                if h % 2 == 0:
                    if h >= 2:
                        pe.wait_ge(s_ltp, h // 2)
                    else:
                        chunk_free(pe, c0("cz1") - 1)
                        chunk_free(pe, c0("cz1"))
                    for i in range(2):
                        for t in range(T):
                            src = qpe[:, t, h:h + 2, :] if i == 0 else kpe[:, t, h:h + 2, :]
                            last = nc.tensor.transpose(G[0][:, i * S + t * P:i * S + t * P + P],
                                                       src.rearrange("p h d -> p (h d)"), ident[:, :])
                last.then_inc(s_lt, 1)

            def mla_score(h):
                pe.wait_ge(s_ltq, h + 1)
                pe.wait_ge(s_ltp, h // 2 + 1)
                if h >= 1:
                    pe.wait_ge(s_lse, h)
                rows_ = slice((h % 2) * 64, (h % 2) * 64 + 64)
                qk, pt = qk_t[:, h % 2, :], pe_t[:, (h // 2) % 2, :]
                for t, (o, kw) in enumerate((((0), P), ((P), S))):
                    mm(A[1][:, o:o + kw], qk[:, t * P:t * P + P], qk[:, S:S + kw], start=True, stop=False)
                    i = mm(A[1][:, o:o + kw], pt[rows_, t * P:t * P + P], pt[rows_, S:S + kw],
                           start=False, stop=True)
                i.then_inc(s_ls, 1)

            def mla_prob_turn(h):
                pe.wait_ge(s_lx, h + 1)
                if h >= 1:
                    pe.wait_ge(s_lpe, h)
                for i in range(3):
                    last = nc.tensor.transpose(A[2][:, i * P:i * P + P], prob[:, h % 2, i * P:i * P + P],
                                               ident[:, :])
                last.then_inc(s_lp, 1)

            def mla_weigh(h):
                pe.wait_ge(s_lpe, h + 1)
                if h >= 1:
                    pe.wait_ge(s_ln, h)
                for i, (t, k) in enumerate(((0, 0), (1, 0), (1, 1))):
                    last = mm(A[3][:, t * P:t * P + P], prob_t[:, h % 2, i * P:i * P + P],
                              kv_c[:, k, h, P:2 * P], start=k == 0, stop=i != 1)
                last.then_inc(s_lo_, 1)

            pe.wait_ge(s_ident, 16)
            for p in range(NPIECES):
                if p == p0("cout"):
                    for e in range(MLA_H + 3):
                        if e >= 3:
                            mla_weigh(e - 3)
                        if 2 <= e < MLA_H + 2:
                            mla_prob_turn(e - 2)
                        if 1 <= e < MLA_H + 1:
                            mla_score(e - 1)
                        if e < MLA_H:
                            mla_turn(e)
                for h in rel_heads(p):
                    rel_rows(h)
                head_weigh(p)
                head_prob_turn(p)
                head_score(p)
                head_turn(p)
                ml_step(p)
                for name, which in turn_steps(p):
                    turn(name, which)
                if p == p0("xp"):
                    gate_logits()
                if p == p0("xp") + 1:
                    gate_rows()
                if p == p0("zp") + 1:
                    gate_cols()
                pool_mix(p)

                for name in ("memkv", "qkv", "wout", "up", "xp", "cu", "uq", "cout"):
                    turned_for = {"memkv": "mem", "qkv": "mix", "wout": "merged", "up": "ffn",
                                  "xp": "ml", "cu": "mla", "uq": "cq", "cout": "o"}
                    if p == p0(name):
                        pe.wait_ge(s_tlo, sum(fills(turned_for[name])[:2]))
                piece_ready(p)
                name = [n for n, *_ in PHASES if p0(n) <= p][-1]
                i_ = p - p0(name)
                r = p % RING
                if name in ("memkv", "qkv", "z", "wout", "xp", "om", "cu", "cz0", "cz1", "cout"):
                    xh, xl = (x1hi, x1lo) if name == "memkv" else (x0hi, x0lo)
                    c = c0(name) + i_ // 2
                    if i_ % 2 == 0:
                        chunk_free(pe, c - 2)
                    i = tokens_piece(p, xh, xl, range(4 * (i_ % 2), 4 * (i_ % 2) + 4),
                                     (bank(c, 0), bank(c, 1)), 352 if name == "cu" else 512,
                                     i_ % 2 == 0, i_ % 2 == 1)
                elif name == "br":
                    c = c0(name) + i_
                    if i_ % 2 == 0:
                        pe.wait_ge(s_tlo, sum(fills(("ya", "yr", "ym")[i_ // 2])[:2]))
                    chunk_free(pe, c - 2)
                    xh, xl = (x0hi, x0lo) if i_ >= 4 else (x1hi, x1lo)
                    kb0 = 4 if i_ // 2 == 1 else 0
                    i = tokens_piece(p, xh, xl, range(kb0, kb0 + 4), (bank(c, 0), bank(c, 1)), 512,
                                     True, True)
                elif name in ("up", "zp", "xm", "zm"):
                    xh, xl = (x1hi, x1lo) if name == "up" else (x0hi, x0lo)
                    c = c0(name) + i_
                    chunk_free(pe, c - 2)
                    for b in range(2):
                        i = channels_block(r, xh, xl, range(KB), b * P, 2 * P,
                                           bank(c)[:, b * S:b * S + S])
                elif name in ("down", "aout"):
                    c = c0(name)
                    if i_ == 0:
                        chunk_free(pe, c - 2)
                        chunk_free(pe, c - 1)
                    if name == "down":
                        pe.wait_ge(s_hlo, i_ + 1)
                        src = [(hthi, htlo, 2 * i_), (hthi, htlo, 2 * i_ + 1)]
                    elif i_ < 4:
                        pe.wait_ge(s_yblo, i_ + 1)
                        src = [(ybhi, yblo, 2 * i_), (ybhi, yblo, 2 * i_ + 1)]
                    else:
                        pe.wait_ge(s_mylo, i_ - 3)
                        src = [(x0hi, x0lo, 2 * (i_ - 4)), (x0hi, x0lo, 2 * (i_ - 4) + 1)]
                    n_ = 11 if name == "down" else 8
                    for t in range(T):
                        ts = slice(t * P, t * P + P)
                        for h in range(2):
                            for j, (xh, xl, kb) in enumerate(src):
                                ws = slice(j * D + h * 512, j * D + h * 512 + 512)
                                i = passes(bank(c + h, t)[:, :], xh[:, kb, ts], xl[:, kb, ts],
                                           whi[:, r, ws], wlo[:, r, ws],
                                           i_ == 0 and j == 0, i_ == n_ - 1 and j == 1)
                elif name in ("pool", "wq", "wk"):
                    for g in range(4):
                        c = c0(name) + g
                        chunk_free(pe, c - 2)
                        if name == "pool":
                            pe.wait_ge(s_mixlo, g + 1)
                            xh, xl = x1hi, x1lo
                        else:
                            pe.wait_ge(s_xclo, 4)
                            xh, xl = x1hi, x1lo
                        for d in range(2):
                            i = channels_block(r, xh, xl, (2 * g, 2 * g + 1), g * 512 + d * P, S,
                                               bank(c)[:, d * S:d * S + S])
                        if g < 3:
                            i.then_inc(s_part, 1)
                elif name == "wv":
                    pe.wait_ge(s_xmlo, 4)
                    for pair in range(2):
                        c = c0(name) + pair
                        chunk_free(pe, c - 2)
                        for t in range(T):
                            for h in (2 * pair, 2 * pair + 1):
                                for j in range(2):
                                    ws = slice(h * 512 + j * S, h * 512 + j * S + S)
                                    o = bank(c, t)[:, (h % 2) * S:(h % 2) * S + S]
                                    ts = slice(t * P, t * P + P)
                                    i = passes(o, xmhi[:, 2 * h + j, ts], xmlo[:, 2 * h + j, ts],
                                               whi[:, r, ws], wlo[:, r, ws], j == 0, j == 1)
                        if pair == 0:
                            i.then_inc(s_part, 1)
                elif name == "uq":
                    c = c0(name) + i_
                    chunk_free(pe, c - 2)
                    i = tokens_piece(p, cqhi, cqlo, range(3), (bank(c, 0), bank(c, 1)), 512, True, True)
                elif name == "ukv":
                    for n in range(2):
                        c = c0(name) + 2 * i_ + n
                        chunk_free(pe, c - 2)
                        for t in range(T):
                            ts = slice(t * P, t * P + P)
                            for j in range(2):
                                ws = slice(j * D + n * 512, j * D + n * 512 + 512)
                                i = passes(bank(c, t)[:, :], cqhi[:, 3 + j, ts], cqlo[:, 3 + j, ts],
                                           whi[:, r, ws], wlo[:, r, ws], j == 0, j == 1)
                        if n == 0:
                            i.then_inc(s_part, 1)
                i.then_inc(s_mm, 1)

        @block.scalar
        def _(act):
            count = [0]

            def order(i):
                count[0] += 1
                i.then_inc(s_act, 1)
                act.wait_ge(s_act, count[0])

            def split(p):
                if p >= NPIECES:
                    return
                act.wait_ge(s_piece[p % RING], 16 * (p // RING + 1))
                if p >= RING:
                    act.wait_ge(s_mm, p - RING + 1)
                nc.scalar.copy(whi[:, p % RING, :], raw[:, p % RING, :]).then_inc(s_hi, 1)

            def squares(name):
                n = SUMS.index(name)
                if name == "mem":
                    act.wait_ge(s_mem, 16)
                if name == "mix":
                    act.wait_ge(s_x, 16)
                    act.wait_ge(s_turn, sum(fills("mem")[:2]))
                if name == "ffn":
                    chunk_free(act, c0("wout") + 1)
                if name == "final":
                    chunk_free(act, c0("down") + 1)
                if name == "ml":
                    act.wait_ge(s_fin, 1)
                if name == "mla":
                    chunk_free(act, c0("aout") + 1)
                if name == "cq":
                    chunk_free(act, c0("cu") + 1)
                    for i, (a, b) in enumerate(((0, 384), (384, 640))):
                        for t in range(T):
                            last = nc.scalar.activation(xn[:, t, a:b], cu[:, t, a:b], ACT.Square,
                                                        accum_out=stats[:, 2 * n + 2 * i + t:2 * n + 2 * i + t + 1])
                else:
                    src = tok[:, 12:14, :, :].rearrange("p a b c -> p (a b c)").rearrange(
                        "p (t d) -> p t d", t=T) if name == "mem" else xres
                    for t in range(T):
                        last = nc.scalar.activation(xn[:, t, :], src[:, t, :], ACT.Square,
                                                    accum_out=stats[:, 2 * n + t:2 * n + t + 1])
                last.then_inc(s_ss, 1)

            FREE = {"ya": p0("qkv"), "yr": p0("qkv"), "ym": p0("br"), "merged": p0("wout"),
                    "ffn": p0("up"), "ml": p0("xp"), "mla": p0("cu"), "cq": p0("cu"),
                    "o": p0("cout")}

            def turn_hi(name, which):
                base, _, kbs = fills(name)
                hi, _, d0 = DEST[name]
                if name in FREE:
                    act.wait_ge(s_mm, FREE[name])
                for i in which:
                    act.wait_ge(s_turn, base + i + 1)
                    b, m = turn_bank(name, i), min(2, kbs - 2 * i)
                    if isinstance(gain(name, 0), float):
                        last = nc.scalar.activation(
                            hi[:, d0 + 2 * i:d0 + 2 * i + 2, :].rearrange("p k s -> p (k s)"), b[:, :],
                            ACT.Copy, scale=gain(name, 0))
                    else:
                        for j in range(m):
                            last = nc.scalar.activation(hi[:, d0 + 2 * i + j, :], b[:, j * S:j * S + S],
                                                        ACT.Copy, scale=gain(name, 2 * i + j))
                    last.then_inc(s_thi, 1)

            def rel_copy(h):
                act.wait_ge(s_rb, h + 1)
                if h >= 2:
                    act.wait_ge(s_rbd[h % 2], 16 * (h // 2))
                nc.scalar.copy(brows[:, h % 2, :], A[3][:, 0:TRI]).then_inc(s_rbs, 1)

            def head_act(p):
                if head_at(p - 2) and head_at(p - 2)[0] != "ret":
                    j = job(*head_at(p - 2))
                    n = SMAX.index(j)
                    w = len((0, 1, 2, 3) if JOBS[j][0] == "mem" else (0, 1, 2)) * P
                    act.wait_ge(s_jp, n + 1)
                    nc.scalar.copy(prob_t[:, n % 2, 0:w], A[2][:, 0:w]).then_inc(s_jpe, 1)
                if head_at(p - 1) and head_at(p - 1)[0] != "ret":
                    kind, h = head_at(p - 1)
                    j = job(kind, h)
                    n = SMAX.index(j)
                    act.wait_ge(s_jse, j + 1)
                    spans = ((0, S), (S, 2 * S)) if kind == "mem" else ((0, P), (P, TRI))
                    for t, (a, b) in enumerate(spans):
                        i = nc.scalar.activation(prob[:, j % 2, a:b], prob[:, j % 2, a:b], ACT.Exp,
                                                 bias=nmax[:, n % 4, t:t + 1], scale=1.0,
                                                 accum_out=psumr[:, n % 4, t:t + 1])
                    i.then_inc(s_jx, 1)

            def ml_act(p):
                e = p - ML0
                if 0 <= e < ML_H:
                    act.wait_ge(s_mw, e + 1)
                    w = prob_t[:, e % 2, :]
                    nc.scalar.activation(w[:, 0:S], w[:, 0:S], ACT.Exp, bias=gcol[:, 0, 0, e:e + 1], scale=1.0)
                    nc.scalar.activation(w[:, S:TRI], w[:, S:TRI], ACT.Exp,
                                         bias=gcol[:, 0, 1, e:e + 1], scale=1.0).then_inc(s_mx, 1)
                if 1 <= e <= ML_H:
                    act.wait_ge(s_hm, e)
                    if e >= 2:
                        act.wait_ge(s_mss, e - 1)
                    for t in range(T):
                        i = nc.scalar.activation(junk[:, :], hm[(e - 1) % 2][:, t, :], ACT.Square,
                                                 accum_out=stats[:, 16 + 2 * (e - 1) + t:17 + 2 * (e - 1) + t])
                        if t == 0:
                            order(i)
                    i.then_inc(s_mss, 1)
                if 4 <= e < 4 + ML_H:
                    h = e - 4
                    act.wait_ge(s_mya, h + 1)
                    act.wait_ge(s_mm, p0("aout"))
                    nc.scalar.activation(x0hi[:, 2 * h:2 * h + 2, :], xc[:, 2 * h:2 * h + 2, :],
                                         ACT.Copy, scale=0.5).then_inc(s_myhi, 1)

            def xc_act(p):
                i = p - p0("xm") - 1
                if 0 <= i < 4:
                    chunk_free(act, c0("xm") + i)
                    if i >= 2:
                        act.wait_ge(s_silu, i - 1)
                    nc.scalar.activation(prob_t[:, i % 2, :],
                                         xc[:, 2 * i:2 * i + 2, :].rearrange("p k s -> p (k s)"),
                                         ACT.Tanh, scale=0.5).then_inc(s_conv, 1)
                i = p - p0("xm") - 2
                if 0 <= i < 4:
                    act.wait_ge(s_silu, i + 1)
                    if i == 0:
                        act.wait_ge(s_mm, p0("xm"))
                    nc.scalar.activation(x1hi[:, 2 * i:2 * i + 2, :], xc[:, 2 * i:2 * i + 2, :],
                                         ACT.Copy, scale=0.5).then_inc(s_fhi, 1)

            def gates_act(p):
                q = p - p0("xp")
                if q == 0:
                    act.wait_ge(s_gm, 1)
                    nc.scalar.copy(gsb[:, :, :], A[0][:, 0:16].rearrange("p (t g) -> p t g", t=T)).then_inc(s_gc, 1)
                if q == 2:
                    act.wait_ge(s_gr, 1)
                    nc.scalar.activation(rows[:, 0, :], rows[:, 2, :], ACT.Exp).then_inc(s_gx, 1)
                    act.wait_ge(s_gx, 1)
                    nc.scalar.activation(rows[:, 0, :], rows[:, 0, :], ACT.Ln, bias=1.0).then_inc(s_gx, 1)
                if q == 4:
                    act.wait_ge(s_gr, 2)
                    nc.scalar.activation(rows[:, 3, :], rows[:, 3, :], ACT.Exp, scale=-1.0).then_inc(s_gx, 1)
                if q == 5:
                    act.wait_ge(s_gct, 1)
                    nc.scalar.copy(gcol[:, :, :, :].rearrange("p a t h -> p (a t h)"),
                                   A[1][:, 0:16]).then_inc(s_gcol, 1)

            def mla_angles():
                act.wait_ge(s_ang, 1)
                nc.scalar.activation(csin[:, :, :], ang[:, 0, :, :], ACT.Sin)
                nc.scalar.activation(ccos[:, :, :], ang[:, 1, :, :], ACT.Sin).then_inc(s_sin, 1)

            def mla_squares(tiles):
                for n in tiles:
                    which, t = divmod(n, 2)
                    if n == 0:
                        chunk_free(act, c0("uq") + 2)
                        act.wait_ge(s_tlo, sum(fills("cq")[:2]))
                    if n == 2:
                        chunk_free(act, c0("ukv") + 3)
                    if n >= 1:
                        act.wait_ge(s_csqr, n)
                    flat = xn[:, :, :].rearrange("p t d -> p (t d)")
                    if which == 0:
                        i = nc.scalar.activation(flat[:, 0:1536].rearrange("p (h d) -> p h d", d=192),
                                                 q_c[:, t, :, :], ACT.Square)
                    else:
                        i = nc.scalar.activation(flat[:, 0:D].rearrange("p (h d) -> p h d", d=P),
                                                 kv_c[:, t, :, 0:P], ACT.Square)
                    i.then_inc(s_csq, 1)

            def mla_head_act(e):
                if 2 <= e < MLA_H + 2:
                    act.wait_ge(s_lp, e - 1)
                    nc.scalar.copy(prob_t[:, e % 2, 0:TRI], A[2][:, 0:TRI]).then_inc(s_lpe, 1)
                if e < MLA_H and e % 2 == 0:
                    act.wait_ge(s_lt, e + 1)
                    nc.scalar.copy(pe_t[:, (e // 2) % 2, :], G[0][:, :]).then_inc(s_ltp, 1)
                if 1 <= e < MLA_H + 1:
                    h = e - 1
                    act.wait_ge(s_lse, h + 1)
                    for t, (a, b) in enumerate(((0, P), (P, TRI))):
                        i = nc.scalar.activation(prob[:, h % 2, a:b], prob[:, h % 2, a:b], ACT.Exp,
                                                 bias=nmax[:, h % 4, t:t + 1], scale=1.0,
                                                 accum_out=psumr[:, h % 4, t:t + 1])
                    i.then_inc(s_lx, 1)

            def empty(p):
                for c, (owner, number, end, part) in enumerate(CHUNKS):
                    if end != p:
                        continue
                    name = [n for n, *_ in PHASES if c0(n) <= c][-1]
                    n = c - c0(name)
                    done = None
                    tanh_to = lambda t: prob_t[:, t, :]
                    if owner == "act" or name in ("up", "xm", "zp", "zm", "cz0", "cz1") or (name, n) == ("qkv", GR):
                        wait_chunk(act, c)
                    if name in ("memkv", "qkv", "z"):
                        slot = {"memkv": (8, 9), "qkv": range(8), "z": (10, 11, 12, 13, 1, 2)}[name][n]
                        if (name, n) == ("qkv", GR):
                            for t in range(T):
                                i = nc.scalar.activation(tok[:, 11, t, :], bank(c, t)[:, :], ACT.Tanh, scale=0.5)
                            i.then_inc(s_tanh, 1)
                            continue
                        if name == "z" and n == 0:
                            act.wait_ge(s_turn, sum(fills("mix")[:2]))
                        if name == "z" and n == 1:
                            chunk_free(act, c0("qkv") + GR)
                        if name == "z" and n == 2:
                            act.wait_ge(s_rot, 1)
                        if name == "z" and n == 4:
                            act.wait_ge(s_jo, MOBA_H)
                        for t in range(T):
                            if name == "z":
                                done = nc.scalar.activation(tok[:, slot, t, :], bank(c, t)[:, :], ACT.Tanh, scale=0.5)
                            else:
                                done = nc.scalar.copy(tok[:, slot, t, :], bank(c, t)[:, :])
                    elif name == "up":
                        kind, i = n % 2, n // 2
                        buf = (gbuf, ubuf)[kind][:, i % 2, :, :]
                        if i >= 2:
                            act.wait_ge(s_hlo, i - 1)
                        for b in range(2):
                            blk = kind * FB + 2 * i + b
                            o = nc.scalar.activation(buf[:, b, :], bank(c)[:, b * S:b * S + S], ACT.Identity,
                                                     bias=pcol("conv_b", blk), scale=pcol("conv_w", 88 + blk))
                        o.then_inc(s_cv, 1)
                    elif name == "xm":
                        for b in range(2):
                            blk = 2 * n + b
                            nc.scalar.activation(xc[:, blk, :], bank(c)[:, b * S:b * S + S], ACT.Identity,
                                                 bias=pcol("a_conv_b", blk), scale=pcol("a_conv_w", 24 + blk))
                        nc.scalar.copy(xmhi[:, 2 * n:2 * n + 2, :].rearrange("p k s -> p (k s)"),
                                       bank(c)[:, :]).then_inc(s_cv, 1)
                    elif name in ("zp", "zm"):
                        dst = prob_t if name == "zp" else pe_t
                        nc.scalar.activation(dst[:, n % 2, :], bank(c)[:, :], ACT.Tanh, scale=0.5).then_inc(s_tanh, 1)
                    elif name in ("cz0", "cz1"):
                        for t in range(T):
                            i = nc.scalar.activation(prob_t[:, t, :], bank(c, t)[:, :], ACT.Tanh, scale=0.5)
                        i.then_inc(s_tanh, 1)
                    elif name == "xp":
                        for t in range(T):
                            done = nc.scalar.copy(xp[:, t, n * 512:n * 512 + 512], bank(c, t)[:, :])
                    elif name == "om":
                        if n == 0:
                            act.wait_ge(s_yblo, 4)
                        for t in range(T):
                            done = nc.scalar.activation(om[:, t, n * 512:n * 512 + 512], bank(c, t)[:, :],
                                                        ACT.Tanh, scale=0.5)
                    elif name == "wv":
                        for t in range(T):
                            done = nc.scalar.copy(v_ml[:, t, n * 512:n * 512 + 512], bank(c, t)[:, :])
                    elif name in ("wq", "wk"):
                        dst = (q_ml if name == "wq" else k_ml)[:, 2 * n:2 * n + 2, :]
                        if name == "wq" and n == 0:
                            act.wait_ge(s_mm, p0("wv") + 1)
                        done = nc.scalar.activation(dst.rearrange("p k s -> p (k s)"), bank(c)[:, :],
                                                    ACT.Copy, scale=1.0 if name == "wq" else 1.0 / 16)
                    elif name == "cu":
                        for t in range(T):
                            done = nc.scalar.copy(cu[:, t, n * 352:n * 352 + 352], bank(c, t)[:, 0:352])
                    elif name == "uq":
                        for t in range(T):
                            done = nc.scalar.copy(q_c[:, t, :, :].rearrange("p h d -> p (h d)")
                                                  [:, n * 512:n * 512 + 512], bank(c, t)[:, :])
                    elif name == "ukv":
                        for t in range(T):
                            done = nc.scalar.copy(kv_c[:, t, :, :].rearrange("p h d -> p (h d)")
                                                  [:, n * 512:n * 512 + 512], bank(c, t)[:, :])
                    if owner == "act":
                        done.then_inc(s_emptied["act"], 1)

            act.wait_ge(s_mem, 16)
            act.dma_start(xres[:, :, :].rearrange("p t d -> p (t d)"), ins["x"]).then_inc(s_x, 16)
            act.dma_start(relb[0:32, :], ins["rel_bias"]).then_inc(s_rel, 16)
            act.dma_start(onehot[:, :], ins["onehot"]).then_inc(s_c1, 16)
            act.dma_start(decay[:, :, :].rearrange("p h n -> p (h n)"), ins["decay"]).then_inc(s_c1, 16)
            act.dma_start(rcos[:, :, :].rearrange("p t n -> p (t n)"), ins["rcos"]).then_inc(s_rc, 16)
            act.dma_start(rsin[:, :, :].rearrange("p t n -> p (t n)"), ins["rsin"]).then_inc(s_rc, 16)
            act.dma_start(wgate[:, :, :].rearrange("p k g -> p (k g)"), ins["wgate"]).then_inc(s_gat, 16)
            act.dma_start(posi[:, :], ins["positions"]).then_inc(s_pos, 16)
            act.wait_ge(s_par, 16)
            act.wait_ge(s_memset, 1)
            squares("mem")
            split(0)
            split(1)
            for p in range(NPIECES):
                split(p + 2)
                for h in rel_heads(p):
                    rel_copy(h)
                head_act(p)
                ml_act(p)
                xc_act(p)
                if p == 20:
                    act.wait_ge(s_gat, 16)
                    nc.scalar.copy(wghi[:, :, :], wgate[:, :, :]).then_inc(s_gh, 1)
                if p == p0("cu") - 1:
                    mla_angles()
                if p == p0("xp"):
                    squares("final")
                for name, step in FRONT.items():
                    if step == p:
                        squares(name)
                for name, which in turn_steps(p):
                    if name in XNORMS and name != "mem" and name not in FRONT:
                        squares(name)
                    turn_hi(name, which)
                    if name == "ffn":
                        act.dma_start(gfin[:, :], ins["gfin"]).then_inc(s_gfin, 16)
                        for dst, src in ((poolb[:, :, :, :].rearrange("p g t s -> p (g t s)"), "poolb"),
                                         (mtri[:, :], "mtri"), (mmla[:, :], "mmla"), (invf[:, :], "invf"),
                                         (sel[:, :, :].rearrange("p h n -> p (h n)"), "sel")):
                            act.dma_start(dst, ins[src]).then_inc(s_c2, 16)
                gates_act(p)
                i = p - p0("up")
                if 0 < i < 23 and i % 2 == 1:
                    chunk_free(act, c0("up") + i - 1)
                    g = gbuf[:, (i // 2) % 2, :, :]
                    nc.scalar.activation(g, g, ACT.Gelu).then_inc(s_gelu, 1)
                if 0 < i < 23 and i % 2 == 0:
                    act.wait_ge(s_h, i // 2)
                    k = i - 2
                    nc.scalar.copy(hthi[:, k:k + 2, :], ubuf[:, (k // 2) % 2, :, :]).then_inc(s_hhi, 1)
                if p0("pool") - 3 <= p <= p0("pool"):
                    b = p - (p0("pool") - 3)
                    act.wait_ge(s_mixm, b + 1)
                    nc.scalar.copy(x1hi[:, 2 * b:2 * b + 2, :].rearrange("p k s -> p (k s)"),
                                   A[2 + b % 2][:, :]).then_inc(s_mixhi, 1)
                if p == p0("pool") + 1:
                    for g in range(4):
                        chunk_free(act, c0("pool") + g)
                        nc.scalar.copy(ybhi[:, 2 * g:2 * g + 2, :].rearrange("p k s -> p (k s)"),
                                       ybt[:, g, :]).then_inc(s_ybhi, 1)
                if p == p0("ukv"):
                    mla_squares((0, 1))
                if p == p0("cz1"):
                    mla_squares((2, 3))
                empty(p)
                if p == p0("cout") - 1:
                    for e in range(MLA_H + 3):
                        mla_head_act(e)

        @block.vector
        def _(dve):
            V = nc.vector
            count = [0]

            def order(i):
                count[0] += 1
                i.then_inc(s_dve, 1)
                dve.wait_ge(s_dve, count[0])

            def split(p):
                if p >= NPIECES:
                    return
                dve.wait_ge(s_hi, p + 1)
                V.tensor_tensor(wlo[:, p % RING, :], raw[:, p % RING, :],
                                whi[:, p % RING, :].bitcast(F32), ALU.subtract).then_inc(s_lo, 1)

            def rsqrt(dst, src, over, w):
                v, u = rs_a[:, 0, 0:w], rs_a[:, 1, 0:w]
                order(V.tensor_scalar(v, src, over, EPS, ALU.mult, ALU.add))
                order(V.tensor_scalar(dst.bitcast(I32), v.bitcast(I32), 1, None, ALU.logical_shift_right))
                order(V.tensor_scalar(dst.bitcast(I32), dst.bitcast(I32), -1.0, float(0x5f3759df),
                                      ALU.mult, ALU.add))
                order(V.tensor_scalar(v, v, -0.5, None, ALU.mult))
                for _ in range(3):
                    order(V.tensor_tensor(u, dst, dst, ALU.mult))
                    order(V.tensor_tensor(u, u, v, ALU.mult))
                    order(V.scalar_tensor_tensor(dst, u, 1.5, dst, ALU.add, ALU.mult))

            def normed(name):
                n = SUMS.index(name)
                dve.wait_ge(s_ss, n + 1)
                if name == "cq":
                    rsqrt(rstd[:, 2 * n:2 * n + 2], stats[:, 2 * n:2 * n + 2], 1.0 / 384, 2)
                    rsqrt(rstd[:, 2 * n + 2:2 * n + 4], stats[:, 2 * n + 2:2 * n + 4], 1.0 / 256, 2)
                    for i, (a, b) in enumerate(((0, 384), (384, 640))):
                        for t in range(T):
                            last = V.tensor_scalar(xn[:, t, a:b], cu[:, t, a:b],
                                                   rstd[:, 2 * n + 2 * i + t:2 * n + 2 * i + t + 1], None, ALU.mult)
                    last.then_inc(s_xn, 1)
                    return
                rsqrt(rstd[:, 2 * n:2 * n + 2], stats[:, 2 * n:2 * n + 2], 1.0 / D, 2)
                src = tok[:, 12:14, :, :].rearrange("p a b c -> p (a b c)").rearrange(
                    "p (t d) -> p t d", t=T) if name == "mem" else xres
                for t in range(T):
                    r = rstd[:, 2 * n + t:2 * n + t + 1]
                    if name == "final":
                        if t == 0:
                            dve.wait_ge(s_gfin, 16)
                        last = V.scalar_tensor_tensor(xres[:, t, :], xres[:, t, :], r, gfin[:, :],
                                                      ALU.mult, ALU.mult)
                    else:
                        last = V.tensor_scalar(xn[:, t, :], src[:, t, :], r, None, ALU.mult)
                last.then_inc(s_fin if name == "final" else s_xn, 1)

            def turn_lo(name, which):
                base, _, kbs = fills(name)
                hi, lo, d0 = DEST[name]
                for i in which:
                    dve.wait_ge(s_thi, base + i + 1)
                    b, m = turn_bank(name, i), min(2, kbs - 2 * i)
                    for j in range(m):
                        if isinstance(gain(name, 0), float):
                            if j:
                                continue
                            k = slice(d0 + 2 * i, d0 + 2 * i + 2)
                            args = (lo[:, k, :].rearrange("p k s -> p (k s)"), b[:, :], gain(name, 0),
                                    hi[:, k, :].rearrange("p k s -> p (k s)").bitcast(F32))
                        else:
                            k = d0 + 2 * i + j
                            args = (lo[:, k, :], b[:, j * S:j * S + S], gain(name, 2 * i + j),
                                    hi[:, k, :].bitcast(F32))
                        last = V.scalar_tensor_tensor(*args, ALU.mult, ALU.subtract)
                    last.then_inc(s_tlo, 1)

            def head_dve(p):
                if head_at(p - 3):
                    kind, h = head_at(p - 3)
                    j = job(kind, h)
                    dve.wait_ge(s_jo, j + 1)
                    if kind == "ret":
                        for t in range(T):
                            i = V.bn_stats(bn[:, t, :], A[3][:, t * P:t * P + P])
                        order(i)
                        for t in range(T):
                            i = V.bn_aggr(mv[:, t, :], bn[:, t, :])
                        order(i)
                        rsqrt(rsum[:, :], mv[:, :, 1], 1.0, T)
                        c = slice(h * P, h * P + P)
                        for t in range(T):
                            i = V.tensor_scalar(tok[:, 3, t, c], A[3][:, t * P:t * P + P], mv[:, t, 0:1],
                                                rsum[:, t:t + 1], ALU.subtract, ALU.mult)
                        order(i)
                        V.tensor_tensor(tok[:, 3, :, c], tok[:, 3, :, c], tok[:, 6, :, c],
                                        ALU.mult).then_inc(s_jn, 1)
                    else:
                        n = SMAX.index(j)
                        order(V.reciprocal(rsum[:, :], psumr[:, n % 4, :]))
                        s_, w = (0, 64) if kind == "moba" else (7, P)
                        for t in range(T):
                            i = V.tensor_scalar(tok[:, s_, t, h * w:h * w + w], A[3][:, t * P:t * P + w],
                                                rsum[:, t:t + 1], None, ALU.mult)
                        i.then_inc(s_jn, 1)
                if head_at(p - 1):
                    kind, h = head_at(p - 1)
                    j = job(kind, h)
                    pr = prob[:, j % 2, :]
                    dve.wait_ge(s_js, j + 1)
                    if kind == "ret":
                        V.tensor_tensor(pr[:, 0:TRI], A[1][:, 0:TRI], decay[:, h, :], ALU.mult).then_inc(s_jse, 1)
                    else:
                        n = SMAX.index(j)
                        if kind == "moba":
                            if h == 0:
                                dve.wait_ge(s_bias, 16 * MOBA_H)
                            V.scalar_tensor_tensor(pr[:, 0:P], A[1][:, 0:P], 0.125, bias[:, h, P:S],
                                                   ALU.mult, ALU.add)
                            order(V.scalar_tensor_tensor(pr[:, P:TRI], A[1][:, P:TRI], 0.125, bias[:, h, :],
                                                         ALU.mult, ALU.add))
                            spans = ((0, P), (P, TRI))
                        else:
                            order(V.tensor_scalar(pr, A[1][:, :], P ** -0.5, None, ALU.mult))
                            spans = ((0, S), (S, 2 * S))
                        for t, (a, b) in enumerate(spans):
                            i = V.tensor_reduce(nmax[:, n % 4, t:t + 1], pr[:, a:b], AX, ALU.max, negate=True)
                        i.then_inc(s_jse, 1)
                if head_at(p) and job(*head_at(p)) in TURNED:
                    n = TURNED.index(job(*head_at(p)))
                    dve.wait_ge(s_jt, n + 1)
                    V.tensor_copy(qk_t[:, n % 2, :], A[0][:, :]).then_inc(s_jte, 1)

            def gates_dve(p):
                q = p - p0("xp")
                if q == 1:
                    dve.wait_ge(s_gt, 1)
                    V.tensor_scalar(rows[:, 1, :], A[1][0:4, 0:S], par[0:4, PCOL["b_i"][0]:PCOL["b_i"][0] + 1],
                                    None, ALU.add)
                    order(V.tensor_scalar(rows[:, 3, :], A[1][0:4, S:2 * S],
                                          par[0:4, PCOL["b_f"][0]:PCOL["b_f"][0] + 1], None, ALU.add))
                    order(V.scalar_tensor_tensor(rows[:, 2, :], rows[:, 3, :], -1.0, rows[:, 3, :],
                                                 ALU.mult, ALU.min))
                    V.tensor_scalar(rows[:, 3, :], rows[:, 3, :], 0.0, None, ALU.min).then_inc(s_gr, 1)
                if q == 3:
                    dve.wait_ge(s_gx, 2)
                    dve.wait_ge(s_zero, 1)
                    order(V.tensor_tensor(rows[:, 3, :], rows[:, 3, :], rows[:, 0, :], ALU.subtract))
                    order(V.tensor_tensor_scan(rows[:, 0, :], rows[:, 3, :], rows[:, 4, :], 0.0, ALU.add, ALU.add))
                    order(V.tensor_tensor(rows[:, 1, :], rows[:, 1, :], rows[:, 0, :], ALU.subtract))
                    order(V.tensor_tensor_scan(rows[:, 2, :], rows[:, 1, :], rows[:, 1, :], 0.0, ALU.max, ALU.max))
                    order(V.tensor_tensor(rows[:, 3, :], rows[:, 0, :], rows[:, 2, :], ALU.add))
                    V.tensor_scalar(rows[:, 2, :], rows[:, 2, :], -1.0, None, ALU.mult).then_inc(s_gr, 1)

            def ml_dve(p):
                e = p - ML0
                if 0 <= e <= ML_H:
                    dve.wait_ge(s_mo, e + 1)
                if 0 <= e < ML_H:
                    w = prob_t[:, e % 2, :]
                    V.tensor_tensor(w[:, 0:S], A[0][:, 0:S], mtri[:, :], ALU.add)
                    V.tensor_tensor(w[:, S:TRI], A[0][:, P:S], mtri[:, 0:P], ALU.add).then_inc(s_mw, 1)
                if 1 <= e <= ML_H:
                    h = e - 1
                    order(V.tensor_copy(rsum[:, :], A[0][:, 400:402]))
                    order(V.scalar_tensor_tensor(rsum[:, :], rsum[:, :], -1.0, rsum[:, :], ALU.mult, ALU.max))
                    order(V.tensor_tensor(rsum[:, :], rsum[:, :], gcol[:, 1, :, h], ALU.max))
                    order(V.reciprocal(rsum[:, :], rsum[:, :]))
                    for t in range(T):
                        i = V.tensor_scalar(hm[h % 2][:, t, :], A[3][:, t * S:t * S + S], rsum[:, t:t + 1],
                                            None, ALU.mult)
                    i.then_inc(s_mh, 1)
                    dve.wait_ge(s_mh, h + 1)
                    V.scalar_tensor_tensor(hm[h % 2], om[:, :, h * S:h * S + S], 1.0, hm[h % 2],
                                           ALU.add, ALU.mult).then_inc(s_hm, 1)
                if 0 <= e < ML_H:
                    dve.wait_ge(s_mx, e + 1)
                    V.tensor_tensor(prob[:, e % 2, 0:TRI], A[1][:, 0:TRI], prob_t[:, e % 2, 0:TRI],
                                    ALU.mult).then_inc(s_mp, 1)
                if 1 <= e <= ML_H:
                    h = e - 1
                    dve.wait_ge(s_mss, h + 1)
                    rsqrt(rstd[:, 16 + 2 * h:18 + 2 * h], stats[:, 16 + 2 * h:18 + 2 * h], 0.25 / S, T)
                    for t in range(T):
                        i = V.tensor_scalar(hm[h % 2][:, t, :], hm[h % 2][:, t, :],
                                            rstd[:, 16 + 2 * h + t:17 + 2 * h + t], 0.5, ALU.mult, ALU.mult)
                    i.then_inc(s_mn, 1)
                if 2 <= e < ML_H + 2:
                    h = e - 2
                    dve.wait_ge(s_mt, h + 1)
                    dve.wait_ge(s_mskip, 1)
                    for j in range(2):
                        blk = 2 * h + j
                        i = V.scalar_tensor_tensor(xc[:, blk, :], A[2][:, j * S:j * S + S], pcol("head_g", blk),
                                                   xc[:, blk, :], ALU.mult, ALU.add)
                    order(i)
                    V.tensor_tensor(xc[:, 2 * h:2 * h + 2, :], xc[:, 2 * h:2 * h + 2, :],
                                    zm[:, 2 * h:2 * h + 2, :], ALU.mult).then_inc(s_mya, 1)
                if 4 <= e < 4 + ML_H:
                    h = e - 4
                    k = slice(2 * h, 2 * h + 2)
                    dve.wait_ge(s_myhi, h + 1)
                    V.scalar_tensor_tensor(x0lo[:, k, :], xc[:, k, :], 0.5, x0hi[:, k, :].bitcast(F32),
                                           ALU.mult, ALU.subtract).then_inc(s_mylo, 1)

            def xc_dve(p):
                i = p - p0("xm") - 1
                if 0 <= i < 4:
                    dve.wait_ge(s_conv, i + 1)
                    k = slice(2 * i, 2 * i + 2)
                    V.scalar_tensor_tensor(xc[:, k, :].rearrange("p k s -> p (k s)"), prob_t[:, i % 2, :], 1.0,
                                           xc[:, k, :].rearrange("p k s -> p (k s)"),
                                           ALU.add, ALU.mult).then_inc(s_silu, 1)
                i = p - p0("xm") - 2
                if 0 <= i < 4:
                    k = slice(2 * i, 2 * i + 2)
                    dve.wait_ge(s_fhi, i + 1)
                    V.scalar_tensor_tensor(x1lo[:, k, :], xc[:, k, :], 0.5, x1hi[:, k, :].bitcast(F32),
                                           ALU.mult, ALU.subtract).then_inc(s_xclo, 1)

            def angles():
                dve.wait_ge(s_pos, 16)
                dve.wait_ge(s_c2, 80)
                order(V.tensor_copy(posf[:, :], posi[:, :]))
                for t in range(T):
                    i = V.tensor_scalar(ang[:, 0, t, :], invf[:, :], posf[:, t:t + 1], None, ALU.mult)
                order(i)
                a, k = ang[:, 0, :, :], ang[:, 1, :, :]
                order(V.tensor_scalar(k, a, 0.15915494309189535, 12582912.0, ALU.mult, ALU.add))
                order(V.tensor_scalar(k, k, -12582912.0, None, ALU.add))
                for c in (6.28125, 0.0019350051879882812, 3.0198365992e-7):
                    order(V.scalar_tensor_tensor(a, k, -c, a, ALU.mult, ALU.add))
                order(V.tensor_scalar(a, a, 3.1415925, -3.1415925, ALU.min, ALU.max))
                order(V.scalar_tensor_tensor(k, a, -1.0, a, ALU.mult, ALU.min))
                V.tensor_scalar(k, k, 1.5707963267948966, None, ALU.add).then_inc(s_ang, 1)

            def mla_pe_k():
                sq = junk[:, 0:P].rearrange("p (t d) -> p t d", t=T)
                dve.wait_ge(s_sin, 1)
                order(V.tensor_tensor(sq, cu[:, :, 640:704], cu[:, :, 640:704], ALU.mult))
                V.tensor_reduce(kpss[:, :], sq, AX, ALU.add)
                kp = PCOL["kn_pe"][0]
                order(V.tensor_tensor(kpr[:, :, :], cu[:, :, 640:704],
                                      par[:, kp:kp + 64].unsqueeze(1).broadcast_to([P, T, 64]), ALU.mult))
                a, b = kpr[:, :, 0:32], kpr[:, :, 32:64]
                t4 = junk[:, :].rearrange("p (n t d) -> p n t d", n=4, t=T)
                V.tensor_tensor(t4[:, 0], a, ccos[:, :, :], ALU.mult)
                V.tensor_tensor(t4[:, 1], b, csin[:, :, :], ALU.mult)
                V.tensor_tensor(t4[:, 2], a, csin[:, :, :], ALU.mult)
                order(V.tensor_tensor(t4[:, 3], b, ccos[:, :, :], ALU.mult))
                V.tensor_tensor(a, t4[:, 0], t4[:, 1], ALU.subtract)
                order(V.tensor_tensor(b, t4[:, 2], t4[:, 3], ALU.add))
            def mla_sums(tiles):
                flat = xn[:, :, :].rearrange("p t d -> p (t d)")
                for n in tiles:
                    which, t = divmod(n, 2)
                    dve.wait_ge(s_csq, n + 1)
                    src = (flat[:, 0:1536].rearrange("p (h d) -> p h d", d=192) if which == 0 else
                           flat[:, 0:D].rearrange("p (h d) -> p h d", d=P))
                    V.tensor_reduce(kss[:, which, t, :], src, AX, ALU.add).then_inc(s_csqr, 1)
            def mla_qk():
                dve.wait_ge(s_csqr, 4)
                for t in range(T):
                    i = V.tensor_scalar(kss[:, 1, t, :], kss[:, 1, t, :], kpss[:, t:t + 1], None, ALU.add)
                order(i)
                for which in range(2):
                    rsqrt(rqk[:, which, :, :].rearrange("p t h -> p (t h)"),
                          kss[:, which, :, :].rearrange("p t h -> p (t h)"), 1.0 / 192, 16)
                V.tensor_scalar(rqk[:, 0, :, :], rqk[:, 0, :, :], 192 ** -0.5, None, ALU.mult)
                for t in range(T):
                    r = rqk[:, 1, t, :].unsqueeze(2)
                    V.tensor_tensor(kpe[:, t, :, :], kpr[:, t, :].unsqueeze(1).broadcast_to([P, MLA_H, 64]),
                                    r.broadcast_to([P, MLA_H, 64]), ALU.mult)
                    i = V.tensor_tensor(kv_c[:, t, :, 0:P], kv_c[:, t, :, 0:P],
                                        r.broadcast_to([P, MLA_H, P]), ALU.mult)
                i.then_inc(s_cqk, 1)

            def mla_head_dve(e):
                if e >= 3:
                    h = e - 3
                    dve.wait_ge(s_lo_, h + 1)
                    order(V.reciprocal(rsum[:, :], psumr[:, h % 4, :]))
                    for t in range(T):
                        i = V.scalar_tensor_tensor(kv_c[:, t, h, 0:P], A[3][:, t * P:t * P + P], rsum[:, t:t + 1],
                                                   cz[:, t, h * P:h * P + P], ALU.mult, ALU.mult)
                    i.then_inc(s_ln, 1)
                if 1 <= e < MLA_H + 1:
                    h = e - 1
                    pr = prob[:, h % 2, :]
                    dve.wait_ge(s_ls, h + 1)
                    for t, (a, b) in enumerate(((0, P), (P, TRI))):
                        i = V.scalar_tensor_tensor(pr[:, a:b], A[1][:, a:b], rqk[:, 0, t, h:h + 1], mmla[:, a:b],
                                                   ALU.mult, ALU.add)
                    order(i)
                    for t, (a, b) in enumerate(((0, P), (P, TRI))):
                        i = V.tensor_reduce(nmax[:, h % 4, t:t + 1], pr[:, a:b], AX, ALU.max, negate=True)
                    i.then_inc(s_lse, 1)
                if e < MLA_H:
                    dve.wait_ge(s_lt, e + 1)
                    V.tensor_scalar(qk_t[:, e % 2, 0:S], A[0][:, 0:S], pcol("qn"), None, ALU.mult)
                    V.tensor_scalar(qk_t[:, e % 2, S:2 * S], A[0][:, S:2 * S], pcol("kn"), None,
                                    ALU.mult).then_inc(s_ltq, 1)

            def taps(c, buf, cols, shifts):
                for s_, col in zip(shifts, cols):
                    for b in range(2):
                        i = V.scalar_tensor_tensor(buf[:, b, s_:S], bank(c)[:, b * S:b * S + S - s_], col(b),
                                                   buf[:, b, s_:S], ALU.mult, ALU.add)
                    if s_ != shifts[-1]:
                        order(i)
                return i

            def empty(p):
                for c, (owner, number, end, part) in enumerate(CHUNKS):
                    if end != p or owner != "dve":
                        continue
                    name = [n for n, *_ in PHASES if c0(n) <= c][-1]
                    n = c - c0(name)
                    wait_chunk(dve, c)
                    if name == "qkv":
                        dve.wait_ge(s_tanh, 1)
                        for t in range(T):
                            i = V.scalar_tensor_tensor(tok[:, 6, t, :], tok[:, 11, t, :], 1.0, bank(c, t)[:, :],
                                                       ALU.add, ALU.mult)
                    elif name == "br":
                        br, half_ = divmod(n, 2)
                        zs = ((10, 11), (12, 13), (1, 2))[br][half_]
                        chunk_free(dve, c0("z") + 2 * br + half_)
                        for t in range(T):
                            i = V.scalar_tensor_tensor(tok[:, zs, t, :], tok[:, zs, t, :], 1.0, bank(c, t)[:, :],
                                                       ALU.add, ALU.mult)
                        if br >= 1:
                            order(i)
                            m = 10 + half_
                            i = V.tensor_tensor(tok[:, m, :, :], tok[:, m, :, :], tok[:, zs, :, :], ALU.add)
                    elif name in ("wout", "down", "aout", "cout"):
                        for t in range(T):
                            x = xres[:, t, n * 512:n * 512 + 512]
                            i = V.tensor_tensor(x, bank(c, t)[:, :], x, ALU.add)
                    elif name == "up":
                        kind, k = n % 2, n // 2
                        dve.wait_ge(s_cv, n + 1)
                        i = taps(c, (gbuf, ubuf)[kind][:, k % 2, :, :],
                                 [lambda b, j=j: pcol("conv_w", j * 44 + kind * FB + 2 * k + b) for j in (1, 0)],
                                 (1, 2))
                    elif name == "xm":
                        dve.wait_ge(s_cv, 22 + n + 1)
                        k = slice(2 * n, 2 * n + 2)
                        V.tensor_tensor(xmlo[:, k, :].rearrange("p k s -> p (k s)"), bank(c)[:, :],
                                        xmhi[:, k, :].rearrange("p k s -> p (k s)").bitcast(F32), ALU.subtract)\
                            .then_inc(s_xmlo, 1)
                        i = taps(c, xc[:, k, :],
                                 [lambda b, j=j: pcol("a_conv_w", j * 8 + 2 * n + b) for j in (2, 1, 0)],
                                 (1, 2, 3))
                    elif name in ("zp", "zm"):
                        dve.wait_ge(s_tanh, (1 if name == "zp" else 5) + n + 1)
                        dst, th = (zp, prob_t) if name == "zp" else (zm, pe_t)
                        i = V.scalar_tensor_tensor(dst[:, 2 * n:2 * n + 2, :].rearrange("p k s -> p (k s)"),
                                                   th[:, n % 2, :], 1.0, bank(c)[:, :], ALU.add, ALU.mult)
                    elif name == "pool":
                        for b in range(2):
                            blk = 2 * n + b
                            i = V.scalar_tensor_tensor(ybt[:, n, b * S:b * S + S], bank(c)[:, b * S:b * S + S],
                                                       hc(4 + blk), zp[:, blk, :], ALU.mult, ALU.mult)
                    elif name in ("cz0", "cz1"):
                        k = int(name == "cz1")
                        dve.wait_ge(s_tanh, 10 + k)
                        for t in range(T):
                            i = V.scalar_tensor_tensor(cz[:, t, k * 512:k * 512 + 512], prob_t[:, t, :], 1.0,
                                                       bank(c, t)[:, :], ALU.add, ALU.mult)
                    i.then_inc(s_emptied["dve"], 1)

            dve.wait_ge(s_par, 16)
            for o, (name, w) in ((0, ("gn", 4)), (4, ("pool_scale", 8)), (12, ("skip", 8))):
                a = PCOL[name][0]
                i = V.tensor_scalar(half[:, o:o + w], par[:, a:a + w], 0.5, None, ALU.mult)
            order(i)
            dve.wait_ge(s_ident, 16)
            normed("mem")
            split(0)
            split(1)
            for p in range(NPIECES):
                split(p + 2)
                head_dve(p)
                ml_dve(p)
                xc_dve(p)
                gates_dve(p)
                if p == 20:
                    dve.wait_ge(s_gh, 1)
                    V.tensor_tensor(wglo[:, :, :], wgate[:, :, :], wghi[:, :, :].bitcast(F32),
                                    ALU.subtract).then_inc(s_gl, 1)
                if p == p0("xp"):
                    normed("final")
                if p == p0("aout") - 1:
                    angles()
                for name, step in FRONT.items():
                    if step == p:
                        normed(name)
                for name, which in turn_steps(p):
                    if name in XNORMS and name != "mem" and name not in FRONT:
                        normed(name)
                    turn_lo(name, which)
                if p0("pool") - 3 <= p <= p0("pool"):
                    b = p - (p0("pool") - 3)
                    dve.wait_ge(s_mixhi, b + 1)
                    V.tensor_tensor(x1lo[:, 2 * b:2 * b + 2, :].rearrange("p k s -> p (k s)"),
                                    A[2 + b % 2][:, :],
                                    x1hi[:, 2 * b:2 * b + 2, :].rearrange("p k s -> p (k s)").bitcast(F32),
                                    ALU.subtract).then_inc(s_mixlo, 1)
                if p == p0("ukv"):
                    mla_pe_k()
                    mla_sums((0, 1))
                if p == p0("cz1"):
                    mla_sums((2, 3))
                    mla_qk()
                empty(p)
                if p == p0("cout") - 1:
                    for e in range(MLA_H + 3):
                        mla_head_dve(e)

        @block.gpsimd
        def _(pool):
            Q = nc.gpsimd
            count = [0]

            def order(i):
                count[0] += 1
                i.then_inc(s_pool, 1)
                pool.wait_ge(s_pool, count[0])

            order(Q.memset(ones[:, :], 1.0))
            Q.memset(relw[32:33, :, :], 1.0).then_inc(s_memset, 1)
            pool.wait_ge(s_memset, 1)
            pool.wait_ge(s_rel, 16)
            for h in range(MOBA_H):
                if h >= 2:
                    pool.wait_ge(s_rb, h - 1)
                Q.tensor_copy(relw[0:32, h % 2, :], relb[0:32, h:h + 1].broadcast_to([32, P])).then_inc(s_rbw, 1)
                if h >= 1:
                    pool.wait_ge(s_rbs, h)
                    pool.dma_start(scratch[h - 1].rearrange("(p n) -> p n", p=P), brows[:, (h - 1) % 2, :])\
                        .then_inc(s_rbd[(h - 1) % 2], 16)
            pool.wait_ge(s_rbs, MOBA_H)
            pool.dma_start(scratch[MOBA_H - 1].rearrange("(p n) -> p n", p=P), brows[:, (MOBA_H - 1) % 2, :])\
                .then_inc(s_rbd[(MOBA_H - 1) % 2], 16)
            for i in range(2):
                pool.wait_ge(s_rbd[i], 16 * MOBA_H // 2)
            for h in range(MOBA_H):
                pool.dma_start(bias[:, h, :], scratch[h, P - 1:P - 1 + P * (TRI - 1)]
                               .rearrange("(p n) -> p n", p=P)[:, 0:S]).then_inc(s_bias, 16)
            pool.wait_ge(s_rc, 32)
            for s_, c in ((3, 3), (4, 4)):
                chunk_free(pool, c0("qkv") + c)
                for t in range(T):
                    v = tok[:, s_, t, :].rearrange("p (h d) -> p h d", h=RET_H)
                    a, b = v[:, :, 0:64], v[:, :, 64:128]
                    cos = rcos[:, t, :].unsqueeze(1).broadcast_to([P, RET_H, 64])
                    sin = rsin[:, t, :].unsqueeze(1).broadcast_to([P, RET_H, 64])
                    tmp = tok[:, 12, :, :].rearrange("p t (n h d) -> p (t n) h d", n=2, h=RET_H)
                    Q.tensor_tensor(tmp[:, 0], a, cos, ALU.mult)
                    Q.tensor_tensor(tmp[:, 1], b, sin, ALU.mult)
                    Q.tensor_tensor(tmp[:, 2], a, sin, ALU.mult)
                    order(Q.tensor_tensor(tmp[:, 3], b, cos, ALU.mult))
                    Q.tensor_tensor(a, tmp[:, 0], tmp[:, 1], ALU.subtract)
                    order(Q.tensor_tensor(b, tmp[:, 2], tmp[:, 3], ALU.add))
            Q.memset(junk[:, :], 0.0).then_inc(s_rot, 1)
            for i in range(11):
                u = ubuf[:, i % 2, :, :]
                pool.wait_ge(s_gelu, i + 1)
                chunk_free(pool, c0("up") + 2 * i + 1)
                Q.tensor_tensor(u, gbuf[:, i % 2, :, :], u, ALU.mult).then_inc(s_h, 1)
                pool.wait_ge(s_hhi, i + 1)
                Q.tensor_tensor(htlo[:, 2 * i:2 * i + 2, :], u, hthi[:, 2 * i:2 * i + 2, :].bitcast(F32),
                                ALU.subtract).then_inc(s_hlo, 1)
            Q.memset(rows[:, 4, :], 0.0).then_inc(s_zero, 1)
            for g in range(4):
                pool.wait_ge(s_ybhi, g + 1)
                k = slice(2 * g, 2 * g + 2)
                Q.tensor_tensor(yblo[:, k, :].rearrange("p k s -> p (k s)"), ybt[:, g, :],
                                ybhi[:, k, :].rearrange("p k s -> p (k s)").bitcast(F32),
                                ALU.subtract).then_inc(s_yblo, 1)
            pool.wait_ge(s_xclo, 4)
            for blk in range(KB):
                i = Q.tensor_scalar(xc[:, blk, :], xc[:, blk, :], hc(12 + blk), None, ALU.mult)
            i.then_inc(s_mskip, 1)
            chunk_free(pool, c0("uq") + 2)
            pool.wait_ge(s_sin, 1)
            qp = PCOL["qn_pe"][0]
            for t in range(T):
                v = qpe[:, t, :, :]
                order(Q.tensor_tensor(v, q_c[:, t, :, P:192],
                                      par[:, qp:qp + 64].unsqueeze(1).broadcast_to([P, MLA_H, 64]), ALU.mult))
                a, b = v[:, :, 0:32], v[:, :, 32:64]
                cos = ccos[:, t, :].unsqueeze(1).broadcast_to([P, MLA_H, 32])
                sin = csin[:, t, :].unsqueeze(1).broadcast_to([P, MLA_H, 32])
                tmp = pe_t[:, :, :].rearrange("p a (n h d) -> p (a n) h d", n=2, h=MLA_H)
                Q.tensor_tensor(tmp[:, 0], a, cos, ALU.mult)
                Q.tensor_tensor(tmp[:, 1], b, sin, ALU.mult)
                Q.tensor_tensor(tmp[:, 2], a, sin, ALU.mult)
                order(Q.tensor_tensor(tmp[:, 3], b, cos, ALU.mult))
                Q.tensor_tensor(a, tmp[:, 0], tmp[:, 1], ALU.subtract)
                i = Q.tensor_tensor(b, tmp[:, 2], tmp[:, 3], ALU.add)
                if t == 0:
                    order(i)
            i.then_inc(s_cpe, 1)


def rel_buckets(d):
    large = 16 + (np.log(np.maximum(d, 1) / 16.0) / np.log(2048 / 16.0) * 16).astype(np.int64)
    return np.where(d < 16, d, np.minimum(large, 31))


def constants():
    f = lambda a: np.ascontiguousarray(a, dtype=np.float32)
    i = np.arange(P)
    onehot = np.zeros((P, TRI), np.float32)
    d = 255 - np.arange(TRI)
    for j in range(TRI):
        if d[j] >= 0:
            onehot[rel_buckets(d[j:j + 1])[0], j] = 1.0
        else:
            onehot[32, j] = NEG
    gamma = np.log1p(-np.power(2.0, -5.0 - np.arange(RET_H)))
    q = np.arange(S)
    diff = q[None, :] - i[:, None]
    dec = np.stack([np.where(diff >= 0, np.exp(g * np.maximum(diff, 0)), 0.0) * RET_SCALE for g in gamma], 1)
    dec = np.concatenate([dec, dec[:, :, 0:P]], -1)
    inv = (10000.0 ** (-np.arange(64, dtype=np.float32) / np.float32(64))).astype(np.float32)
    ang = (q.astype(np.float32)[:, None] * inv).astype(np.float64)
    to_tiles = lambda a: a.reshape(T, P, -1).transpose(1, 0, 2).reshape(P, -1)
    poolb = np.zeros((P, 4, T, S))
    for g, w in enumerate((2, 4, 8, 16)):
        for st in range(T):
            s_ = st * P + i[:, None]
            t = q[None, :]
            poolb[:, g, st, :] = ((s_ <= t) & (s_ > t - w)) / np.minimum(t + 1, w) - (s_ == t)
    mtri = np.where(q[None, :] < i[:, None], NEG, 0.0)
    block_ = np.where((i[:, None] // 64) >= (i[None, :] // 64), 0.0, NEG)
    mmla = np.concatenate([block_, np.zeros((P, P)), block_], 1)
    inv2 = (10000.0 ** (-np.arange(0, 64, 2, dtype=np.float32) / np.float32(64))).astype(np.float32)
    sel = np.zeros((P, ML_H, P))
    for h in range(ML_H):
        sel[h, h, :] = 1.0
    return {"ident": f(np.eye(P)), "onehot": onehot, "decay": f(dec.reshape(P, -1)),
            "rcos": f(to_tiles(np.cos(ang))), "rsin": f(to_tiles(np.sin(ang))),
            "poolb": f(poolb.reshape(P, -1)), "mtri": f(mtri), "mmla": f(mmla),
            "invf": f(np.repeat(inv2[None], P, 0)), "sel": f(sel.reshape(P, -1))}


RET_SCALE = 128 ** -0.5


def lay_out(a):
    pieces = []

    def add(w, kbs, cols):
        blocks = [w[k * P:k * P + P, cols] for k in kbs]
        m = np.concatenate(blocks, 1)
        pieces.append(np.pad(m, ((0, 0), (0, PIECE - m.shape[1]))))

    def halves(w, col, n, width=512):
        for c in range(n):
            for h in range(2):
                add(w, range(4 * h, 4 * h + 4), slice(col + c * width, col + c * width + width))

    w_in, w_up, a_in, c_in = a["w_in"][0], a["w_up"][0], a["a_w_in_2"][0], a["c_w_in_2"][0]
    halves(a["w_mem_kv"][0], 0, 2)
    halves(w_in, 0, 14)
    for n in ("w_br_attn", "w_br_ret", "w_br_mem"):
        for c in range(2):
            add(a[n][0], range(4), slice(c * 512, c * 512 + 512))
    halves(a["w_out"][0], 0, 2)
    for i in range(11):
        for k in range(2):
            add(w_up, range(8), slice(k * FF + i * S, k * FF + i * S + S))
    for i in range(11):
        add(a["w_down"][0], (2 * i, 2 * i + 1), slice(0, D))
    gates = 2 * D
    XP = gates + 8 + D

    def quarters(col):
        for i in range(4):
            add(a_in, range(8), slice(col + i * S, col + i * S + S))

    halves(a_in, XP, 2)
    quarters(XP + D)
    heads = lambda w: pieces.append(w.reshape(4, 2, P, S).transpose(2, 0, 1, 3).reshape(P, PIECE))
    heads(a["a_pool_w_2"][0])
    quarters(0)
    halves(a_in, D, 2)
    heads(a["a_w_v_2"][0])
    heads(a["a_w_q_2"][0])
    heads(a["a_w_k_2"][0])
    quarters(gates + 8)
    for i in (4, 5, 6, 7, 0, 1, 2, 3):
        add(a["a_w_out_2"][0], (2 * i, 2 * i + 1), slice(0, D))
    halves(c_in, 0, 2, 352)
    halves(c_in, 704, 1)
    for c in range(3):
        add(a["c_w_uq_2"][0], range(3), slice(c * 512, c * 512 + 512))
    for c in range(2):
        add(a["c_w_ukv_2"][0], range(2), slice(c * D, c * D + D))
    halves(c_in, 704 + 512, 1)
    halves(a["c_w_out_2"][0], 0, 2)
    assert len(pieces) == NPIECES, (len(pieces), NPIECES)

    cols = lambda v: v.reshape(-1, P).T
    wide = lambda v: np.repeat(v[None], P, 0)
    four = lambda v: np.pad(v.reshape(4, 1), ((0, P - 4), (0, 0)))
    par = {"g_mem": cols(a["g_mem"]), "g_mix": cols(a["g_mix"]), "gn": cols(a["ret_gn_gain"]),
           "g_ffn": cols(a["g_ffn"]), "conv_w": cols(a["conv_w"]), "conv_b": cols(a["conv_b"]),
           "a_norm": cols(a["a_norm_g_2"]), "a_conv_w": cols(a["a_conv_w_2"]),
           "a_conv_b": cols(a["a_conv_b_2"]), "head_g": cols(a["a_head_norm_g_2"]),
           "skip": cols(a["a_skip_2"]), "pool_scale": cols(a["a_pool_scale_2"]),
           "c_norm": cols(a["c_norm_g_2"]),
           "cqkv_norm": np.concatenate([cols(a["c_q_norm_g_2"]), cols(a["c_kv_norm_g_2"])], 1),
           "qn": cols(a["c_qn_g_2"][0, 0:P]), "kn": cols(a["c_kn_g_2"][0, 0:P]),
           "qn_pe": wide(a["c_qn_g_2"][0, P:192]), "kn_pe": wide(a["c_kn_g_2"][0, P:192]),
           "b_i": four(a["a_b_if_2"][0, 0:4]), "b_f": four(a["a_b_if_2"][0, 4:8])}
    tiles = lambda v: v.reshape(T, P, -1).transpose(1, 0, 2).reshape(P, -1)
    arrays = {"weights": np.stack(pieces), "params": np.concatenate([par[n] for n in PCOL], 1),
              "x": tiles(a["x"][0]), "mem": tiles(a["mem"][0]), "rel_bias": a["rel_bias"],
              "gfin": wide(a["g_final"]),
              "wgate": a_in[:, gates:gates + 8].reshape(KB, P, 8).transpose(1, 0, 2).reshape(P, -1),
              "positions": a["positions_2"].reshape(T, P).T}
    return arrays


def kernel(**inputs):
    import concourse.bacc as _bacc
    from concourse.bass_utils import run_bass_kernel_spmd as _run

    arrays = lay_out({n: np.asarray(v) for n, v in inputs.items()})
    arrays.update(constants())
    arrays = {n: np.ascontiguousarray(v) for n, v in arrays.items()}
    nc = _bacc.Bacc("TRN2", target_bir_lowering=False, num_devices=1)
    ins = {n: nc.dram_tensor(f"in_{n}", v.shape, mybir.dt.from_np(v.dtype), kind="ExternalInput").ap()
           for n, v in arrays.items()}
    out = nc.dram_tensor("out_x", (S, D), F32, kind="ExternalOutput").ap()
    program(nc, ins, out)
    r = _run(nc, [{f"in_{n}": v for n, v in arrays.items()}], core_ids=[0])
    return r.results[0]["out_x"].reshape(1, S, D)
```
